# Optimizing a Trainium2 kernel written in Bass

```python
import jax, jax.numpy as jnp
from jax import lax
import numpy as np

D_MODEL = 1024
BATCH = 1
SEQ = 256
DEPTH = 2

N_MIXERS = 2
N_ATTN_LAYERS = (DEPTH + 1) // 2
N_GDN_LAYERS = DEPTH // 2
D_FF = 2816
NORM_EPS = 1e-6

ATTN_Q_HEADS = 16
ATTN_KV_HEADS = 4
ATTN_HEAD_DIM = 64
ATTN_GROUP = ATTN_Q_HEADS // ATTN_KV_HEADS
WINDOW = 128
ATTN_BLOCK = 128
ROPE_DIM = ATTN_HEAD_DIM // 4
ROPE_THETA = 500000.0
ATTN_Q_W = ATTN_Q_HEADS * ATTN_HEAD_DIM
ATTN_KV_W = ATTN_KV_HEADS * ATTN_HEAD_DIM
ATTN_IN = ATTN_Q_W + 2 * ATTN_KV_W

GDN_HEADS = 8
GDN_DK = 128
GDN_DV = 128
GDN_CONV = 4
GDN_CHUNK = 64
GDN_QK_W = GDN_HEADS * GDN_DK
GDN_V_W = GDN_HEADS * GDN_DV
GDN_CONV_W = 2 * GDN_QK_W + GDN_V_W
GDN_IN = GDN_CONV_W + GDN_V_W + 2 * GDN_HEADS

kernel_name = "hybrid_swa_sink_gdn_macaron"

def rms_norm(x, w):
    xf = x.astype(jnp.float32)
    y = xf * lax.rsqrt(jnp.mean(xf * xf, axis=-1, keepdims=True) + NORM_EPS)
    return (y * w.astype(jnp.float32)).astype(x.dtype)

def swiglu_ffn(h, w_gate_up, w_down):
    gate, up = jnp.split(h @ w_gate_up, 2, axis=-1)
    return (jax.nn.silu(gate) * up) @ w_down

def partial_rope(t, cos, sin):
    tf = t.astype(jnp.float32)
    half = ROPE_DIM // 2
    r1, r2, rest = tf[..., :half], tf[..., half:ROPE_DIM], tf[..., ROPE_DIM:]
    out = jnp.concatenate([r1 * cos - r2 * sin, r2 * cos + r1 * sin, rest], axis=-1)
    return out.astype(t.dtype)

def swa_sink_attention(h, cos, sin, w_in, b_in, sinks, w_out, b_out):
    B, S, _ = h.shape
    nb = S // ATTN_BLOCK
    qkv = h @ w_in + b_in
    q, k, v = jnp.split(qkv, [ATTN_Q_W, ATTN_Q_W + ATTN_KV_W], axis=-1)
    q = partial_rope(q.reshape(B, S, ATTN_Q_HEADS, ATTN_HEAD_DIM), cos, sin)
    k = partial_rope(k.reshape(B, S, ATTN_KV_HEADS, ATTN_HEAD_DIM), cos, sin)
    v = v.reshape(B, S, ATTN_KV_HEADS, ATTN_HEAD_DIM)
    qb = q.reshape(B, nb, ATTN_BLOCK, ATTN_KV_HEADS, ATTN_GROUP, ATTN_HEAD_DIM)

    def band(t):
        cur = t.reshape(B, nb, ATTN_BLOCK, ATTN_KV_HEADS, ATTN_HEAD_DIM)
        prev = jnp.pad(cur, ((0, 0), (1, 0), (0, 0), (0, 0), (0, 0)))[:, :-1]
        return jnp.concatenate([prev, cur], axis=2)

    kb, vb = band(k), band(v)
    scores = jnp.einsum('bnqhgd,bnkhd->bnhgqk', qb, kb,
                        preferred_element_type=jnp.float32) * (ATTN_HEAD_DIM ** -0.5)
    qi = jnp.arange(ATTN_BLOCK)[:, None]
    kj = jnp.arange(2 * ATTN_BLOCK)[None, :]
    rel = qi + ATTN_BLOCK - kj
    in_window = (rel >= 0) & (rel < WINDOW)
    blk = jnp.arange(nb)[:, None, None]
    valid = in_window[None] & ((blk - 1) * ATTN_BLOCK + kj[None] >= 0)
    scores = jnp.where(valid[None, :, None, None], scores, -jnp.inf)
    sink = sinks.astype(jnp.float32).reshape(ATTN_KV_HEADS, ATTN_GROUP)[None, None, :, :, None, None]
    m = jnp.maximum(jnp.max(scores, axis=-1, keepdims=True), sink)
    p = jnp.exp(scores - m)
    probs = (p / (jnp.sum(p, axis=-1, keepdims=True) + jnp.exp(sink - m))).astype(v.dtype)
    o = jnp.einsum('bnhgqk,bnkhd->bnqhgd', probs, vb).reshape(B, S, ATTN_Q_W)
    return o @ w_out + b_out

def l2_normalize(t):
    return t * lax.rsqrt(jnp.sum(t * t, axis=-1, keepdims=True) + NORM_EPS)

def chunk_gated_delta_rule(q, k, v, g, beta):
    B, S, H, DK = q.shape
    DV = v.shape[-1]
    C = GDN_CHUNK
    N = S // C

    def to_chunks(t):
        return jnp.moveaxis(t.reshape(B, N, C, H, *t.shape[3:]), 3, 1)

    q, k, v, g, beta = (to_chunks(t) for t in (q, k, v, g, beta))
    decay = jnp.cumsum(g, axis=-1)
    causal = jnp.tril(jnp.ones((C, C), dtype=bool))
    strict = jnp.tril(jnp.ones((C, C), dtype=bool), -1)
    L = jnp.exp(jnp.where(causal, decay[..., :, None] - decay[..., None, :], -jnp.inf))
    k_beta = k * beta[..., None]
    A = jnp.where(strict, jnp.einsum('bhncd,bhnsd->bhncs', k_beta, k) * L, 0.0)
    eye = jnp.eye(C, dtype=jnp.float32)
    rhs = jnp.concatenate([v * beta[..., None], k_beta * jnp.exp(decay)[..., None]], axis=-1)
    sol = lax.linalg.triangular_solve(eye + A, rhs, left_side=True, lower=True)
    U, W = sol[..., :DV], sol[..., DV:]
    Aqk = jnp.where(causal, jnp.einsum('bhncd,bhnsd->bhncs', q, k) * L, 0.0)
    decay_last = decay[..., -1:]
    q_dec = q * jnp.exp(decay)[..., None]
    k_dec = k * jnp.exp(decay_last - decay)[..., None]
    chunk_decay = jnp.exp(decay_last[..., 0])
    xs = tuple(jnp.moveaxis(t, 2, 0) for t in (q_dec, k_dec, U, W, Aqk, chunk_decay))

    def step(state, inp):
        qd, kd, u, w, aqk, cd = inp
        v_new = u - jnp.einsum('bhcd,bhde->bhce', w, state)
        o = jnp.einsum('bhcd,bhde->bhce', qd, state) + jnp.einsum('bhcs,bhse->bhce', aqk, v_new)
        state = state * cd[..., None, None] + jnp.einsum('bhcd,bhce->bhde', kd, v_new)
        return state, o

    _, o = lax.scan(step, jnp.zeros((B, H, DK, DV), jnp.float32), xs)
    return jnp.transpose(o, (1, 0, 3, 2, 4)).reshape(B, S, H, DV)

def gated_deltanet(h, w_in, conv_w, A_log, dt_bias, norm_w, w_out):
    B, S, _ = h.shape
    proj = h @ w_in
    qkv, z, b, a = jnp.split(proj, [GDN_CONV_W, GDN_CONV_W + GDN_V_W, GDN_CONV_W + GDN_V_W + GDN_HEADS], axis=-1)
    qkv = lax.conv_general_dilated(qkv, conv_w[:, None, :].astype(qkv.dtype), window_strides=(1,),
                                   padding=[(GDN_CONV - 1, 0)], dimension_numbers=('NWC', 'WIO', 'NWC'),
                                   feature_group_count=GDN_CONV_W)
    qkv = jax.nn.silu(qkv).astype(jnp.float32)
    q, k, v = jnp.split(qkv, [GDN_QK_W, 2 * GDN_QK_W], axis=-1)
    q = l2_normalize(q.reshape(B, S, GDN_HEADS, GDN_DK)) * (GDN_DK ** -0.5)
    k = l2_normalize(k.reshape(B, S, GDN_HEADS, GDN_DK))
    v = v.reshape(B, S, GDN_HEADS, GDN_DV)
    beta = jax.nn.sigmoid(b.astype(jnp.float32))
    g = -jnp.exp(A_log.astype(jnp.float32)) * jax.nn.softplus(a.astype(jnp.float32) + dt_bias.astype(jnp.float32))
    o = chunk_gated_delta_rule(q, k, v, g, beta)
    zf = z.reshape(B, S, GDN_HEADS, GDN_DV).astype(jnp.float32)
    o = o * lax.rsqrt(jnp.mean(o * o, axis=-1, keepdims=True) + NORM_EPS) * norm_w.astype(jnp.float32) * jax.nn.silu(zf)
    return o.astype(h.dtype).reshape(B, S, GDN_V_W) @ w_out

def setup_inputs(seed: int = 0) -> dict:
    key = jax.random.key(seed)
    ks = jax.random.split(key, 24)
    f32 = jnp.float32

    def nrm(k, shape, fan_in):
        return jax.random.normal(k, shape, f32) * (fan_in ** -0.5)

    def gain(k, shape):
        return 1.0 + 0.05 * jax.random.normal(k, shape, f32)

    x = jax.random.normal(ks[0], (BATCH, SEQ, D_MODEL), f32)
    positions = (jnp.arange(SEQ, dtype=jnp.int32)[None, :]
                 + jax.random.randint(ks[1], (BATCH, 1), 0, 4096, dtype=jnp.int32))
    dt = jnp.exp(jax.random.uniform(ks[17], (N_GDN_LAYERS, GDN_HEADS), f32, np.log(1e-3), np.log(1e-1)))
    return {
        "x": x,
        "positions": positions,
        "ffn1_norm": gain(ks[2], (DEPTH, D_MODEL)),
        "ffn1_w_gate_up": nrm(ks[3], (DEPTH, D_MODEL, 2 * D_FF), D_MODEL),
        "ffn1_w_down": nrm(ks[4], (DEPTH, D_FF, D_MODEL), D_FF),
        "mix_norm": gain(ks[5], (DEPTH, D_MODEL)),
        "ffn2_norm": gain(ks[6], (DEPTH, D_MODEL)),
        "ffn2_w_gate_up": nrm(ks[7], (DEPTH, D_MODEL, 2 * D_FF), D_MODEL),
        "ffn2_w_down": nrm(ks[8], (DEPTH, D_FF, D_MODEL), D_FF),
        "attn_w_in": nrm(ks[9], (N_ATTN_LAYERS, D_MODEL, ATTN_IN), D_MODEL),
        "attn_b_in": 0.02 * jax.random.normal(ks[10], (N_ATTN_LAYERS, ATTN_IN), f32),
        "attn_sinks": jax.random.normal(ks[11], (N_ATTN_LAYERS, ATTN_Q_HEADS), f32),
        "attn_w_out": nrm(ks[12], (N_ATTN_LAYERS, ATTN_Q_W, D_MODEL), ATTN_Q_W),
        "attn_b_out": 0.02 * jax.random.normal(ks[13], (N_ATTN_LAYERS, D_MODEL), f32),
        "gdn_w_in": nrm(ks[14], (N_GDN_LAYERS, D_MODEL, GDN_IN), D_MODEL),
        "gdn_conv_w": nrm(ks[15], (N_GDN_LAYERS, GDN_CONV, GDN_CONV_W), GDN_CONV),
        "gdn_A_log": jnp.log(jax.random.uniform(ks[16], (N_GDN_LAYERS, GDN_HEADS), f32, 1.0, 16.0)),
        "gdn_dt_bias": dt + jnp.log(-jnp.expm1(-dt)),
        "gdn_norm_w": gain(ks[18], (N_GDN_LAYERS, GDN_DV)),
        "gdn_w_out": nrm(ks[19], (N_GDN_LAYERS, GDN_V_W, D_MODEL), GDN_V_W),
        "final_norm": gain(ks[20], (D_MODEL,)),
    }

def reference(x, positions, ffn1_norm, ffn1_w_gate_up, ffn1_w_down, mix_norm, ffn2_norm,
              ffn2_w_gate_up, ffn2_w_down, attn_w_in, attn_b_in, attn_sinks, attn_w_out,
              attn_b_out, gdn_w_in, gdn_conv_w, gdn_A_log, gdn_dt_bias, gdn_norm_w, gdn_w_out,
              final_norm):
    inv_freq = ROPE_THETA ** (-jnp.arange(0, ROPE_DIM, 2, dtype=jnp.float32) / ROPE_DIM)
    ang = positions.astype(jnp.float32)[..., None] * inv_freq
    cos, sin = jnp.cos(ang)[:, :, None, :], jnp.sin(ang)[:, :, None, :]
    h = x
    for layer in range(DEPTH):
        h = h + 0.5 * swiglu_ffn(rms_norm(h, ffn1_norm[layer]), ffn1_w_gate_up[layer], ffn1_w_down[layer])
        hn = rms_norm(h, mix_norm[layer])
        j = layer // N_MIXERS
        if layer % N_MIXERS == 0:
            h = h + swa_sink_attention(hn, cos, sin, attn_w_in[j], attn_b_in[j], attn_sinks[j],
                                       attn_w_out[j], attn_b_out[j])
        else:
            h = h + gated_deltanet(hn, gdn_w_in[j], gdn_conv_w[j], gdn_A_log[j], gdn_dt_bias[j],
                                   gdn_norm_w[j], gdn_w_out[j])
        h = h + 0.5 * swiglu_ffn(rms_norm(h, ffn2_norm[layer]), ffn2_w_gate_up[layer], ffn2_w_down[layer])
    return rms_norm(h, final_norm)


_drawn_inputs = setup_inputs


def setup_inputs(seed=0):
    import zlib

    import numpy as np

    out = dict(_drawn_inputs(seed))
    spreads = {}
    factors = {'gdn_norm_w': 2.681}
    for name, (base, spread) in spreads.items():
        noise = np.random.default_rng([zlib.crc32(name.encode()), seed]).standard_normal(out[name].shape)
        drawn = base * np.exp(spread * noise) if base else spread * noise
        out[name] = __import__('jax').numpy.asarray(drawn.astype(out[name].dtype))
    for name, factor in factors.items():
        out[name] = (out[name] * factor).astype(out[name].dtype)
    return out
```

```python
from contextlib import ExitStack

import numpy as np

import concourse.bass as bass
from concourse import mybir

ALU = mybir.AluOpType
ACT = mybir.ActivationFunctionType
F32 = mybir.dt.float32
F32R = mybir.dt.float32r
I32 = mybir.dt.int32
AX = mybir.AxisListType.X

P = 128
D = 1024
SEQ = 256
TT = SEQ // P
KT = D // P
DFF = 2816
FC = 256
NCH = DFF // FC
EPS = 1e-6
BANK = 512
UNIT = 2048
RING = 4

HQ, HKV, DH = 16, 4, 64
PAIRS = HQ // 2
ROT = 8
THETA = 500000.0
MASKED = -1e30

GH, DK = 8, 128
HG = 4
NG = GH // HG
CONV = 4
LEVELS = [2, 4, 8, 16, 32, 64]

GU_UNITS = 2 * NCH
DOWN_UNITS = DFF // (2 * P)
FFN_UNITS = GU_UNITS + DOWN_UNITS
ATT_IN_UNITS, OUT_UNITS = 6, D // (2 * P)
GDN_IN_UNITS = 4 * NG * 2

U_FFN = [0] * 4
U_FFN[0] = 0
U_ATT = U_FFN[0] + FFN_UNITS
U_ATT_OUT = U_ATT + ATT_IN_UNITS
U_FFN[1] = U_ATT_OUT + OUT_UNITS
U_FFN[2] = U_FFN[1] + FFN_UNITS
U_GDN = U_FFN[2] + FFN_UNITS
U_GDN_OUT = U_GDN + GDN_IN_UNITS
U_FFN[3] = U_GDN_OUT + OUT_UNITS
U_END = U_FFN[3] + FFN_UNITS

E_FFN, E_ATT, E_GDN = [0, 2, 3, 5], 1, 4
GDN_COLS = [part * D + g * HG * DK for g in range(NG) for part in range(4)]
ATT_COLS = [D, 0, BANK]


A_LOADS = G_LOADS = 4
GATE_G = 7
RSTD_FFN, RSTD_ATT, RSTD_GDN, RSTD_FINAL = [1, 3, 4, 7], 2, 4, 7
RESIDUAL_UNIT = [U_ATT, U_FFN[1], U_FFN[2], U_GDN, U_FFN[3], U_END]

ATT_BANKS = [(6, 7), (0, 1), (2, 3)]
ITEMS = [(t, p) for t in range(TT) for p in range(PAIRS)]
FILLS = [(0, (2 * n, 2 * n + 1)) for n in range(HKV)] + [(1, (PAIRS + p,)) for p in range(PAIRS)]
ITEM_FILL = [n for n, (_, items) in enumerate(FILLS) for _ in items]
OT_STEP = [PAIRS + 3, 2 * PAIRS + 2]
OT_PV = [(HKV // 2, HKV), (HKV + PAIRS // 2, HKV + PAIRS)]

CONV_BANKS = [(0, 1), (2, 3), (6, 7)]
R_BANK, KK_BANK, QK_BANK = [2, 3], [6, 0], [7, 1]
Y_BANK, Z_BANK, ZT_BANK = [2, 3], [6, 0], [7, 1]
U_BANK, O_BANK, W_BANK, S_BANK, QS_BANK = [2, 0], [7, 3], 3, 6, 1
RHO, RK = 12, 13
FILLS_G = 14

TWO_PI = 2 * np.pi
TURN = [6.28125, 0.001935302734375, TWO_PI - 6.28125 - 0.001935302734375]
ROUND = 12582912.0
PI_BELOW = 3.1415925
INV_FREQ = THETA ** (-np.arange(0, 2 * ROT, 2, dtype=np.float32) / (2 * ROT))


def build(nc, x, positions, ffn1_norm, ffn1_w_gate_up, ffn1_w_down, mix_norm, ffn2_norm,
          ffn2_w_gate_up, ffn2_w_down, attn_w_in, attn_b_in, attn_sinks, attn_w_out, attn_b_out,
          gdn_w_in, gdn_conv_w, gdn_A_log, gdn_dt_bias, gdn_norm_w, gdn_w_out, final_norm, out):
    ctx = ExitStack()
    with ctx:
        def sb(name, shape, dt=F32, where=ctx):
            return where.enter_context(nc.sbuf_tensor(name, shape, dt))

        def sem(name):
            return ctx.enter_context(nc.semaphore(name))

        x_sb = sb("x_sb", [P, TT, D])
        xT_hi = sb("xT_hi", [P, KT, SEQ], F32R)
        xT_lo = sb("xT_lo", [P, KT, SEQ], F32R)
        w_raw = [sb(f"w_raw{i}", [P, UNIT]) for i in range(RING)]
        w_hi = [sb(f"w_hi{i}", [P, UNIT], F32R) for i in range(RING)]
        w_lo = [sb(f"w_lo{i}", [P, UNIT], F32R) for i in range(RING)]
        ident = sb("ident", [P, P])
        norm_rows = sb("norm_rows", [P, P])
        norm_cols = sb("norm_cols", [P, P])
        conv_rows = sb("conv_rows", [P, P])
        conv_cols = sb("conv_cols", [P, P])
        ssq = sb("ssq", [P, TT])
        mean_sq = sb("mean_sq", [P, TT])
        inv_ms = sb("inv_ms", [P, TT])
        rstd = sb("rstd", [P, TT])

        with ExitStack() as ffn_mem:
            hT_hi = sb("hT_hi", [P, DFF // P * SEQ], F32R, ffn_mem)
            hT_lo = sb("hT_lo", [P, DFF // P * SEQ], F32R, ffn_mem)
            silu_g = [sb(f"silu_g{i}", [P, TT, FC], F32, ffn_mem) for i in range(2)]
            h_row = [sb(f"h_row{i}", [P, TT, FC], F32, ffn_mem) for i in range(2)]
            final_w = sb("final_w", [P, D], F32, ffn_mem)
            y_sb = sb("y_sb", [P, TT, D], F32, ffn_mem)

        with ExitStack() as att_mem:
            a_oT_hi = sb("a_oT_hi", [P, KT, SEQ], F32R, att_mem)
            a_oT_lo = sb("a_oT_lo", [P, KT, SEQ], F32R, att_mem)
            b_in = sb("b_in", [P, 3 * BANK], F32, att_mem)
            b_out = sb("b_out", [P, D], F32, att_mem)
            sink = sb("sink", [P, HQ], F32, att_mem)
            nsink = sb("nsink", [P, HQ], F32, att_mem)
            k_pad = [sb(f"k_pad{t}", [P, HKV, 2, P], F32, att_mem) for t in range(TT)]
            v_pad = [sb(f"v_pad{t}", [P, HKV, 2, P], F32, att_mem) for t in range(TT)]
            kzT = sb("kzT", [P, HKV, 2, SEQ], F32, att_mem)
            q_row = sb("q_row", [P, 2, TT, BANK], F32, att_mem)
            qT = sb("qT", [P, PAIRS, SEQ], F32, att_mem)
            score_mask = sb("score_mask", [P, 2, P], F32, att_mem)
            prob = [sb(f"prob{i}", [P, 2, SEQ], F32, att_mem) for i in range(3)]
            probT = [sb(f"probT{i}", [P, BANK], F32, att_mem) for i in range(2)]
            sm_max = sb("sm_max", [P, TT * PAIRS, 2], F32, att_mem)
            sm_nmax = sb("sm_nmax", [P, TT * PAIRS, 2], F32, att_mem)
            sm_off = sb("sm_off", [P, TT * PAIRS, 2], F32, att_mem)
            sm_sink = sb("sm_sink", [P, TT * PAIRS, 2], F32, att_mem)
            sm_sum = sb("sm_sum", [P, TT * PAIRS, 2], F32, att_mem)
            sm_total = sb("sm_total", [P, TT * PAIRS, 2], F32, att_mem)
            sm_inv = sb("sm_inv", [P, TT * PAIRS, 2], F32, att_mem)
            pos_i = sb("pos_i", [P, TT], I32, att_mem)
            pos_f = sb("pos_f", [P, TT], F32, att_mem)
            invf = sb("invf", [P, 8, ROT], F32, att_mem)
            ang = sb("ang", [P, 2, TT, 8 * ROT], F32, att_mem)
            turns = sb("turns", [P, 2, TT, 8 * ROT], F32, att_mem)
            sincos = sb("sincos", [P, 2, TT, 8, ROT], F32, att_mem)
            rot = [sb(f"rot{i}", [P, 8, ROT], F32, att_mem) for i in range(4)]

        with ExitStack() as gdn_mem:
            g_oT_hi = sb("g_oT_hi", [P, KT, SEQ], F32R, gdn_mem)
            g_oT_lo = sb("g_oT_lo", [P, KT, SEQ], F32R, gdn_mem)
            gates = sb("gates", [P, 10, TT, GH], F32, gdn_mem)
            head_vec = sb("head_vec", [P, 3, GH], F32, gdn_mem)
            norm_w = sb("norm_w", [P, DK], F32, gdn_mem)
            cT = [sb(f"{n}_T", [P, HG, SEQ], F32, gdn_mem) for n in "qkv"]
            v_beta = sb("v_beta", [P, TT, HG, DK], F32, gdn_mem)
            k_dec = sb("k_dec", [P, HG, DK], F32, gdn_mem)
            k_w = sb("k_w", [P, HG, DK], F32, gdn_mem)
            z_gate = sb("z_gate", [P, TT, HG, DK], F32, gdn_mem)
            lower = sb("lower", [P, P], F32, gdn_mem)
            upper = sb("upper", [P, P], F32, gdn_mem)
            ones = sb("ones", [P, P], F32, gdn_mem)
            level = {b: sb(f"level{b}", [P, P], F32, gdn_mem) for b in [1] + LEVELS}
            AqkT = [sb(f"AqkT{t}", [P, HG, P], F32, gdn_mem) for t in range(TT)]
            sc = sb("sc", [P, 14, TT, HG], F32, gdn_mem)
            with ExitStack() as early:
                xs = sb("xs", [P, TT, D], F32, early)
                wba = sb("wba", [P, KT, 2 * GH], F32, early)
                wba_hi = sb("wba_hi", [P, KT, P], F32R, early)
                wba_lo = sb("wba_lo", [P, KT, P], F32R, early)
                ba_T = sb("ba_T", [P, SEQ], F32, early)
            with ExitStack() as late:
                gU = sb("gU", [P, TT, HG, P], F32, late)
                Lm = [sb(f"Lm{t}", [P, HG, P], F32, late) for t in range(TT)]
                AT = [sb(f"AT{t}", [P, HG, P], F32, late) for t in range(TT)]
                Y = [sb(f"Y{t}", [P, HG, P], F32, late) for t in range(TT)]
                X = [sb(f"X{t}", [P, HG, P], F32, late) for t in range(TT)]
                XT = [sb(f"XT{t}", [P, HG, P], F32, late) for t in range(TT)]

        bank = [ctx.enter_context(nc.psum_tensor(f"bank{i}", [P, BANK], F32)) for i in range(8)]
        ENTER_BANKS = [4, 2]
        ACC = [(6, 7), (0, 1)]
        GATE_UP = [(6, 7), (0, 1), (2, 3)]

        def gu_banks(j):
            return GATE_UP[0] if j == 0 else GATE_UP[1] if j % 2 else GATE_UP[2]

        raw_loaded = [sem(f"raw_loaded{i}") for i in range(RING)]
        hi_ready = sem("hi_ready")
        split_ready = sem("split_ready")
        unit_done = sem("unit_done")
        x_loaded = [sem(f"x_loaded{t}") for t in range(TT)]
        rows_zero = sem("rows_zero")
        rows_loaded = sem("rows_loaded")
        ident_ready = sem("ident_ready")
        cols_psum = sem("cols_psum")
        cols_ready = sem("cols_ready")
        resid_ready = sem("resid_ready")
        xs_ready = sem("xs_ready")
        xT_psum = sem("xT_psum")
        xT_hi_ready = sem("xT_hi_ready")
        xT_lo_ready = sem("xT_lo_ready")
        ssq_ready = sem("ssq_ready")
        inv_ready = sem("inv_ready")
        rstd_ready = sem("rstd_ready")
        vec_step = sem("vec_step")
        act_step = sem("act_step")
        pool_step = sem("pool_step")
        acc0_done = sem("acc0_done")
        silu_ready = sem("silu_ready")
        h_ready = sem("h_ready")
        hT_psum = sem("hT_psum")
        hT_hi_ready = sem("hT_hi_ready")
        hT_lo_ready = sem("hT_lo_ready")
        a_loaded = sem("a_loaded")
        a_mask = sem("a_mask")
        a_zero = sem("a_zero")
        bias_added = sem("bias_added")
        angle_ready = sem("angle_ready")
        rope_ready = sem("rope_ready")
        k_row = sem("k_row")
        v_row = sem("v_row")
        q_biased = sem("q_biased")
        k_rot = sem("k_rot")
        v_both = sem("v_both")
        q_rot = sem("q_rot")
        a_fill = sem("a_fill")
        a_evac = sem("a_evac")
        score_done = sem("score_done")
        score_read = sem("score_read")
        max_ready = sem("max_ready")
        exp_done = sem("exp_done")
        prob_ready = sem("prob_ready")
        pv_done = sem("pv_done")
        o_hi_ready = sem("o_hi_ready")
        o_lo_ready = sem("o_lo_ready")
        g_loaded = sem("g_loaded")
        g_masks = sem("g_masks")
        wba_zero = sem("wba_zero")
        wba_hi_ready = sem("wba_hi_ready")
        wba_ready = sem("wba_ready")
        ba_psum = sem("ba_psum")
        ba_ready = sem("ba_ready")
        gate_dve = sem("gate_dve")
        gate_act = sem("gate_act")
        dec_psum = sem("dec_psum")
        conv_first = sem("conv_first")
        conv_sum = sem("conv_sum")
        conv_ready = sem("conv_ready")
        z_silu = sem("z_silu")
        z_ready = sem("z_ready")
        g_fill = sem("g_fill")
        g_evac_act = sem("g_evac_act")
        g_evac_vec = sem("g_evac_vec")
        kq_inv = sem("kq_inv")
        kq_root = sem("kq_root")
        o_inv = sem("o_inv")
        o_root = sem("o_root")
        kq_ssq = sem("kq_ssq")
        gU_ready = sem("gU_ready")
        R_psum = sem("R_psum")
        decay_diff = sem("decay_diff")
        decay_exp = sem("decay_exp")
        L_ready = sem("L_ready")
        KK_psum = sem("KK_psum")
        QK_psum = sem("QK_psum")
        A_ready = sem("A_ready")
        Aqk_ready = sem("Aqk_ready")
        X_ready = sem("X_ready")
        XT_ready = sem("XT_ready")
        Y_psum = sem("Y_psum")
        Y_ready = sem("Y_ready")
        Z_psum = sem("Z_psum")
        ZT_psum = sem("ZT_psum")
        U_psum = sem("U_psum")
        U_ready = sem("U_ready")
        W_psum = sem("W_psum")
        W_ready = sem("W_ready")
        S_psum = sem("S_psum")
        S_ready = sem("S_ready")
        QS_psum = sem("QS_psum")
        QS_ready = sem("QS_ready")
        O_psum = sem("O_psum")
        O_ready = sem("O_ready")
        O_ssq = sem("O_ssq")
        O_final = sem("O_final")
        final_loaded = sem("final_loaded")
        y_ready = sem("y_ready")
        out_stored = sem("out_stored")
        def rounds(eng, f, body):
            if f == 0:
                body(0)
            with eng.Fori(1 if f == 0 else 0, (NCH - 1) // 2) as i:
                body(i)

        def looped(i):
            return not isinstance(i, int)

        block = ctx.enter_context(nc.Block())

        def raw_wait(u0, i):
            return 32 * (u0 // RING + 1) + 32 * i

        @block.sync
        def _(sp):
            def load(u0, i, src):
                if u0 >= RING or looped(i):
                    sp.wait_ge(split_ready, u0 - RING + 1 + 4 * i)
                for half in range(2):
                    dst, s = src(half)
                    sp.dma_start(dst(w_raw[u0 % RING]), s).then_inc(raw_loaded[u0 % RING], 16)

            def gate_up(u0, i, w, kh, c):
                v = w.rearrange("(h t p) (g c n) -> h g c p t n", h=2, t=4, p=P, g=2, c=NCH)
                load(u0, i, lambda g: (
                    lambda raw: raw[:].rearrange("p (t g n) -> p t g n", t=4, g=2)[:, :, g, :], v[kh, g, c]))

            def rows(u0, w, d):
                v = w.rearrange("(d t p) n -> d t p n", t=2, p=P)
                load(u0, 0, lambda t: (lambda raw: raw[:, t * D:(t + 1) * D], v[d, t]))

            def columns(u0, w, kh, col):
                v = w.rearrange("(h s t p) n -> h s p t n", h=2, s=2, t=2, p=P)
                load(u0, 0, lambda s: (
                    lambda raw: raw[:, s * D:(s + 1) * D].rearrange("p (t n) -> p t n", t=2),
                    v[kh, s][:, :, col:col + BANK]))

            def ffn(f, w_gu, w_down):
                u = U_FFN[f]
                for kh in range(2):
                    gate_up(u + kh, 0, w_gu, kh, 0)

                def two_chunks(i):
                    for c in range(2):
                        for kh in range(2):
                            gate_up(u + 2 + 2 * c + kh, i, w_gu, kh, 2 * i + 1 + c)

                rounds(sp, f, two_chunks)
                for d in range(DOWN_UNITS):
                    rows(u + GU_UNITS + d, w_down, d)

            for t in range(TT):
                sp.dma_start(x_sb[:, t, :], x[0, t * P:(t + 1) * P, :]).then_inc(x_loaded[t], 16)
            ffn(0, ffn1_w_gate_up[0], ffn1_w_down[0])
            for n, col in enumerate(ATT_COLS):
                for kh in range(2):
                    columns(U_ATT + 2 * n + kh, attn_w_in[0], kh, col)
            for d in range(OUT_UNITS):
                rows(U_ATT_OUT + d, attn_w_out[0], d)
            ffn(1, ffn2_w_gate_up[0], ffn2_w_down[0])
            ffn(2, ffn1_w_gate_up[1], ffn1_w_down[1])
            for n, col in enumerate(GDN_COLS):
                for kh in range(2):
                    columns(U_GDN + 2 * n + kh, gdn_w_in[0], kh, col)
            for d in range(OUT_UNITS):
                rows(U_GDN_OUT + d, gdn_w_out[0], d)
            ffn(3, ffn2_w_gate_up[1], ffn2_w_down[1])
            for t in range(TT):
                sp.wait_ge(y_ready, t + 1)
                sp.dma_start(out[0, t * P:(t + 1) * P, :], y_sb[:, t, :]).then_inc(out_stored, 16)
            sp.wait_ge(out_stored, 16 * TT)

        @block.gpsimd
        def _(pool):
            steps = [0]

            def after(ins):
                steps[0] += 1
                ins.then_inc(pool_step, 1)
                pool.wait_ge(pool_step, steps[0])

            pool.memset(norm_rows[:], 0.0)
            pool.memset(conv_rows[:], 0.0).then_inc(rows_zero, 1)
            after(pool.memset(ident[:], 0.0))
            pool.affine_select(ident[:], ident[:], pattern=[[-1, P]], compare_op=ALU.not_equal, fill=1.0,
                               base=0, channel_multiplier=1).then_inc(ident_ready, 1)

            pool.wait_ge(unit_done, U_ATT)
            for t in range(TT):
                pool.memset(k_pad[t][:], 0.0)
                z = pool.memset(v_pad[t][:], 0.0)
            z.then_inc(a_zero, 1)
            after(pool.memset(score_mask[:], 0.0))
            pool.affine_select(score_mask[:, 0, :], score_mask[:, 0, :], pattern=[[1, P]],
                               compare_op=ALU.is_gt, fill=MASKED, base=0, channel_multiplier=-1)
            pool.affine_select(score_mask[:, 1, :], score_mask[:, 1, :], pattern=[[-1, P]],
                               compare_op=ALU.is_ge, fill=MASKED, base=0,
                               channel_multiplier=1).then_inc(a_mask, 1)

            def rotate(v, t, heads):
                r1, r2 = v[:, :, 0:ROT], v[:, :, ROT:2 * ROT]
                sin, cos = sincos[:, 0, t, 0:heads, :], sincos[:, 1, t, 0:heads, :]
                m = [r[:, 0:heads, :] for r in rot]
                pool.tensor_tensor(m[0], r1, cos, ALU.mult)
                pool.tensor_tensor(m[1], r2, sin, ALU.mult)
                pool.tensor_tensor(m[2], r2, cos, ALU.mult)
                after(pool.tensor_tensor(m[3], r1, sin, ALU.mult))
                pool.tensor_tensor(r1, m[0], m[1], ALU.subtract)
                return pool.tensor_tensor(r2, m[2], m[3], ALU.add)

            pool.wait_ge(rope_ready, 1)
            for t in range(TT):
                pool.wait_ge(k_row, t + 1)
                after(rotate(k_pad[t][:, :, 0, 0:DH], t, HKV))
                pool.tensor_copy(k_pad[t][:, :, 1, DH:P], k_pad[t][:, :, 0, 0:DH]).then_inc(k_rot, 1)
                pool.wait_ge(v_row, t + 1)
                pool.tensor_copy(v_pad[t][:, :, 1, DH:P], v_pad[t][:, :, 0, 0:DH]).then_inc(v_both, 1)
            for c in range(2):
                for t in range(TT):
                    pool.wait_ge(q_biased, 2 * c + t + 1)
                    rotate(q_row[:, c, t, :].rearrange("p (h d) -> p h d", d=DH), t,
                           BANK // DH).then_inc(q_rot, 1)
                    pool.wait_ge(q_rot, 2 * c + t + 1)
            pool.wait_ge(a_loaded, 16 * A_LOADS)
            for t in range(TT):
                pool.wait_ge(xT_psum, 4 * E_ATT + 4)
                pool.wait_ge(ssq_ready, TT * (E_ATT + 1))
                pool.tensor_tensor(x_sb[:, t, :], x_sb[:, t, :], b_out[:], ALU.add).then_inc(bias_added, 1)

            pool.wait_ge(unit_done, U_GDN)
            pool.memset(wba_hi[:].bitcast(F32), 0.0)
            pool.memset(wba_lo[:].bitcast(F32), 0.0).then_inc(wba_zero, 1)
            pool.memset(ones[:], 1.0)
            pool.memset(lower[:], 1.0)
            after(pool.memset(upper[:], 1.0))
            pool.affine_select(lower[:], lower[:], pattern=[[-1, P]], compare_op=ALU.is_ge, fill=0.0,
                               base=0, channel_multiplier=1)
            pool.affine_select(upper[:], upper[:], pattern=[[1, P]], compare_op=ALU.is_ge, fill=0.0,
                               base=0, channel_multiplier=-1)
            for b in [1] + LEVELS:
                z = pool.memset(level[b][:], 0.0)
            after(z)
            for b in [1] + LEVELS:
                z = pool.memset(level[b][:].rearrange("p (n h b) -> p n h b", h=2, b=b)[:, :, 0, :], 1.0)
            after(z)
            for b in [1] + LEVELS:
                v = level[b][:].rearrange("p (n h b) -> p n h b", h=2, b=b)[:, :, 0, :]
                z = pool.affine_select(v, v, pattern=[[-2 * b, P // (2 * b)], [0, b]], compare_op=ALU.is_ge,
                                       fill=0.0, base=-b, channel_multiplier=1)
            after(z)
            for b in [1] + LEVELS:
                v = level[b][:].rearrange("p (n h b) -> p n h b", h=2, b=b)[:, :, 0, :]
                z = pool.affine_select(v, v, pattern=[[2 * b, P // (2 * b)], [0, b]], compare_op=ALU.is_ge,
                                       fill=0.0, base=2 * b - 1, channel_multiplier=-1)
            z.then_inc(g_masks, 1)

            for g in range(NG):
                if g == 0:
                    pool.wait_ge(gate_dve, GATE_G)
                if g:
                    pool.wait_ge(R_psum, TT * g)
                for t in range(TT):
                    for h in range(HG):
                        z = pool.tensor_scalar(gU[:, t, h, :], upper[:], gates[:, 1, t, HG * g + h:HG * g + h + 1],
                                               None, ALU.mult)
                    z.then_inc(gU_ready, 1)
                pool.wait_ge(g_loaded, 16 * G_LOADS)
                for t in range(TT):
                    pool.wait_ge(z_silu, TT * g + t + 1)
                    pool.tensor_tensor(z_gate[:, t], z_gate[:, t],
                                       norm_w[:].unsqueeze(1).broadcast_to([P, HG, DK]),
                                       ALU.mult).then_inc(z_ready, 1)
                for t in range(TT):
                    pool.wait_ge(decay_exp, TT * g + t + 1)
                    pool.tensor_tensor(Lm[t][:], Lm[t][:], lower[:].unsqueeze(1).broadcast_to([P, HG, P]),
                                       ALU.mult).then_inc(L_ready, 1)


        @block.scalar
        def _(act):
            steps = [0]

            def split_hi(u0, i=0):
                act.wait_ge(raw_loaded[u0 % RING], raw_wait(u0, i))
                if u0 >= RING:
                    act.wait_ge(unit_done, u0 - RING + 1 + 4 * i)
                act.activation(w_hi[u0 % RING][:], w_raw[u0 % RING][:], ACT.Copy).then_inc(hi_ready, 1)

            def square(e, t, src, junk):
                act.activation(junk, src, ACT.Square, accum_out=ssq[:, t:t + 1]).then_inc(ssq_ready, 1)

            def root(n, cols=slice(0, TT)):
                act.wait_ge(inv_ready, n)
                act.activation(rstd[:, cols], inv_ms[:, cols], ACT.Sqrt).then_inc(rstd_ready, 1)

            def enter_hi(e, t):
                for half in range(2):
                    act.wait_ge(xT_psum, 4 * e + 2 * t + half + 1)
                    for j in range(4):
                        kt = 4 * half + j
                        z = act.activation(xT_hi[:, kt, t * P:(t + 1) * P],
                                           bank[ENTER_BANKS[t] + half][:, j * P:(j + 1) * P], ACT.Copy,
                                           scale=norm_cols[:, e * KT + kt:e * KT + kt + 1])
                    z.then_inc(xT_hi_ready, 1)

            def hT_hi_part(f, j, i):
                act.wait_ge(hT_psum, NCH * f + j + 1 + 2 * i)
                act.activation(hT_hi[:, bass.ds((j + 2 * i) * BANK, BANK)], bank[4 + j % 2][:],
                               ACT.Copy).then_inc(hT_hi_ready, 1)

            def gate_chunk(f, j, i, before):
                u, c = U_FFN[f] + 2 * j, NCH * f + j
                act.wait_ge(unit_done, u + 2 + 4 * i)
                for t in range(TT):
                    if c >= 2 or looped(i):
                        act.wait_ge(h_ready, 2 * (c - 2) + t + 1 + 4 * i)
                    act.activation(silu_g[j % 2][:, t, :], bank[gu_banks(j)[t]][:, 0:FC], ACT.Silu,
                                   scale=rstd[:, t:t + 1]).then_inc(silu_ready, 1)
                split_hi(u + 4, i)
                if before:
                    hT_hi_part(f, j - 1, i)
                split_hi(u + 5, i)

            def ffn(f):
                e, u = E_FFN[f], U_FFN[f]
                for t in range(TT):
                    enter_hi(e, t)
                for t in range(TT):
                    square(e, t, x_sb[:, t, :], y_sb[:, t, :])
                if f:
                    split_hi(u + RING - 1)
                else:
                    for n in range(1, RING):
                        split_hi(n)
                root(RSTD_FFN[f])
                act.wait_ge(rstd_ready, RSTD_FFN[f])
                gate_chunk(f, 0, 0, False)

                def two_chunks(i):
                    gate_chunk(f, 1, i, True)
                    gate_chunk(f, 2, i, True)

                rounds(act, f, two_chunks)
                for d in range(DOWN_UNITS - 1):
                    if u + GU_UNITS + d + RING < U_END:
                        split_hi(u + GU_UNITS + d + RING)
                    if d == 0:
                        hT_hi_part(f, NCH - 1, 0)

            act.wait_ge(rows_zero, 1)
            for e, row in enumerate([ffn1_norm[0], mix_norm[0], ffn2_norm[0], ffn1_norm[1], mix_norm[1],
                                     ffn2_norm[1]]):
                act.dma_start(norm_rows[e * KT:(e + 1) * KT, :],
                              row.rearrange("(t p) -> t p", p=P)).then_inc(rows_loaded, 16)
            act.dma_start(conv_rows[0:96, :],
                          gdn_conv_w[0].rearrange("j (t p) -> (j t) p", p=P)).then_inc(rows_loaded, 16)
            act.wait_ge(cols_psum, 1)
            act.activation(norm_cols[:], bank[0][:, 0:P], ACT.Copy)
            act.activation(conv_cols[:], bank[0][:, P:2 * P], ACT.Copy).then_inc(cols_ready, 1)
            act.wait_ge(cols_ready, 1)
            split_hi(0)
            ffn(0)

            act.wait_ge(unit_done, U_ATT)
            act.dma_start(b_in[:], attn_b_in[0:1, :].broadcast_to([P, 3 * BANK])).then_inc(a_loaded, 16)
            act.dma_start(b_out[:], attn_b_out[0:1, :].broadcast_to([P, D])).then_inc(a_loaded, 16)
            act.dma_start(sink[:], attn_sinks[0:1, :].broadcast_to([P, HQ])).then_inc(a_loaded, 16)
            act.dma_start(pos_i[:], positions.rearrange("o (t p) -> p (o t)", p=P),
                          allow_slow_non_contiguous=True).then_inc(a_loaded, 16)
            for t in range(TT):
                enter_hi(E_ATT, t)
            for t in range(TT):
                square(E_ATT, t, x_sb[:, t, :], q_row[:, t].rearrange("p t n -> p (t n)"))
            split_hi(U_ATT + RING - 1)
            root(RSTD_ATT)
            act.wait_ge(angle_ready, 1)
            act.activation(sincos[:].rearrange("p s t h r -> p (s t h r)"),
                           ang[:].rearrange("p s t a -> p (s t a)"), ACT.Sin).then_inc(rope_ready, 1)

            def att_evac(f, dst, src):
                act.wait_ge(a_fill, f + 1)
                act.activation(dst, src, ACT.Copy).then_inc(a_evac, 1)

            split_hi(U_ATT + 4)
            split_hi(U_ATT + 5)
            for f in range(4):
                t, half = f // 2, f % 2
                att_evac(f, kzT[:, 2 * half:2 * half + 2, :, t * P:(t + 1) * P],
                         bank[4 + f % 2][:].rearrange("p (k e n) -> p k e n", k=2, e=2))
            split_hi(U_ATT + 6)
            split_hi(U_ATT + 7)
            for f in range(4, 8):
                c, t = (f - 4) // 2, f % 2
                att_evac(f, qT[:, 4 * c:4 * c + 4, t * P:(t + 1) * P],
                         bank[4 + f % 2][:].rearrange("p (k n) -> p k n", k=4))
                if f == 5:
                    split_hi(U_ATT + 8)
                    split_hi(U_ATT + 9)

            for s in range(len(ITEMS) + 3):
                if s < len(ITEMS):
                    t, p = ITEMS[s]
                    keys = (t + 1) * P
                    pr = prob[s % 3]
                    act.wait_ge(max_ready, s + 1)
                    for h in range(2):
                        act.activation(pr[:, h, 0:keys], pr[:, h, 0:keys], ACT.Exp,
                                       bias=sm_nmax[:, s, h:h + 1], accum_out=sm_sum[:, s, h:h + 1])
                    act.activation(sm_sink[:, s, :], sm_off[:, s, :], ACT.Exp).then_inc(exp_done, 1)
                for n, (t, items) in enumerate(FILLS):
                    if items[-1] == s - 2:
                        if n >= 2:
                            act.wait_ge(pv_done, n - 1)
                        att_evac(8 + n, probT[n % 2][:], bank[4 + n % 2][:])
                for t in range(TT):
                    if s == OT_STEP[t]:
                        for half in range(2):
                            act.wait_ge(pv_done, OT_PV[t][half])
                            act.activation(a_oT_hi[:, 4 * half:4 * half + 4, t * P:(t + 1) * P],
                                           bank[2 * t + half][:].rearrange("p (k n) -> p k n", k=4),
                                           ACT.Copy).then_inc(o_hi_ready, 1)
            for d in range(OUT_UNITS - 1):
                split_hi(U_ATT_OUT + d + RING)
            ffn(1)
            ffn(2)

            act.wait_ge(unit_done, U_GDN)
            act.dma_start(wba[:], gdn_w_in[0].rearrange("(t p) n -> p t n", p=P)[:, :, 4 * D:4 * D + 2 * GH]
                          ).then_inc(g_loaded, 16)
            act.dma_start(head_vec[:, 0, :], gdn_A_log[0:1, :].broadcast_to([P, GH])).then_inc(g_loaded, 16)
            act.dma_start(head_vec[:, 1, :], gdn_dt_bias[0:1, :].broadcast_to([P, GH])).then_inc(g_loaded, 16)
            act.dma_start(norm_w[:], gdn_norm_w[0:1, :].broadcast_to([P, DK])).then_inc(g_loaded, 16)
            for t in range(TT):
                act.wait_ge(resid_ready, 4 * (E_GDN - 1) + 2 * t + 2)
                square(E_GDN, t, x_sb[:, t, :], xs[:, t, :])
                root(RSTD_GDN + t + 1, slice(t, t + 1))
            for t in range(TT):
                enter_hi(E_GDN, t)
            split_hi(U_GDN + RING - 1)
            act.wait_ge(wba_zero, 1)
            act.wait_ge(g_loaded, 16 * G_LOADS)
            act.activation(wba_hi[:, :, 0:2 * GH], wba[:], ACT.Copy).then_inc(wba_hi_ready, 1)

            def conv(g, part):
                n = 4 * g + part
                act.wait_ge(unit_done, U_GDN + 2 * n + 2)
                for b in range(2):
                    for h in (2 * b, 2 * b + 1):
                        col = (CONV - 1) * 24 + part * 8 + HG * g + h
                        z = act.activation(cT[part][:, h, :], bank[CONV_BANKS[part][b]][:, (h % 2) * SEQ:(h % 2 + 1) * SEQ],
                                           ACT.Copy, scale=conv_cols[:, col:col + 1])
                    z.then_inc(conv_first, 1)
                split_hi(U_GDN + 2 * n + 4)
                act.wait_ge(conv_sum, HG * (3 * g + part + 1))
                act.activation(cT[part][:], cT[part][:], ACT.Silu).then_inc(conv_ready, 1)
                split_hi(U_GDN + 2 * n + 5)

            def squares(g, f, row, signal):
                t = f % 2
                act.wait_ge(g_fill, FILLS_G * g + f + 1)
                for h in range(HG):
                    z = act.activation(Lm[t][:, h, :], bank[4 + f % 2][:, h * DK:(h + 1) * DK], ACT.Square,
                                       accum_out=sc[:, row, t, h:h + 1])
                z.then_inc(signal, 1)

            def g_copy(g, f, dst):
                act.wait_ge(g_fill, FILLS_G * g + f + 1)
                act.activation(dst, bank[4 + f % 2][:].rearrange("p (h n) -> p h n", h=HG),
                               ACT.Copy).then_inc(g_evac_act, 1)

            def copy(ready, value, dst, b, signal):
                act.wait_ge(ready, value)
                act.activation(dst, bank[b][:].rearrange("p (h n) -> p h n", h=HG), ACT.Copy).then_inc(signal, 1)

            for g in range(NG):
                conv(g, 0)
                if g == 0:
                    act.wait_ge(ba_psum, 1)
                    act.activation(ba_T[:], bank[6][:, 0:SEQ], ACT.Copy).then_inc(ba_ready, 1)
                    act.wait_ge(gate_dve, 3)
                    act.activation(gates[:, 7], gates[:, 0], ACT.Exp, scale=-1.0).then_inc(gate_act, 1)
                    act.activation(gates[:, 8], gates[:, 6], ACT.Exp).then_inc(gate_act, 1)
                    act.activation(head_vec[:, 2, :], head_vec[:, 0, :], ACT.Exp).then_inc(gate_act, 1)
                    act.wait_ge(gate_act, 3)
                    act.activation(gates[:, 9], gates[:, 8], ACT.Ln, bias=1.0).then_inc(gate_act, 1)
                    act.wait_ge(gate_dve, 9)
                    act.activation(gates[:, 3], gates[:, 2], ACT.Exp).then_inc(gate_act, 1)
                    act.activation(gates[:, 4], gates[:, 5], ACT.Exp).then_inc(gate_act, 1)
                conv(g, 1)
                for t in range(TT):
                    squares(g, t, 0, g_evac_act)
                conv(g, 2)
                for t in range(TT):
                    squares(g, 2 + t, 1, kq_ssq)
                act.wait_ge(kq_inv, g + 1)
                act.activation(sc[:, RHO:RK + 1], sc[:, 2:4], ACT.Sqrt).then_inc(kq_root, 1)
                n = 4 * g + 3
                act.wait_ge(unit_done, U_GDN + 2 * n + 2)
                for t in range(TT):
                    if g:
                        act.wait_ge(O_final, TT * g)
                    act.activation(z_gate[:, t], bank[t][:].rearrange("p (h n) -> p h n", h=HG),
                                   ACT.Silu).then_inc(z_silu, 1)
                split_hi(U_GDN + 2 * n + 4)
                split_hi(U_GDN + 2 * n + 5)
                for t in range(TT):
                    act.wait_ge(decay_diff, TT * g + t + 1)
                    act.activation(Lm[t][:], Lm[t][:], ACT.Exp, scale=-1.0).then_inc(decay_exp, 1)
                for t in range(TT):
                    g_copy(g, 6 + t, AT[t][:])
                for t in range(TT):
                    g_copy(g, 8 + t, XT[t][:])
                for t in range(TT):
                    g_copy(g, 10 + t, AqkT[t][:])
                copy(U_psum, TT * g + 1, Y[0][:], U_BANK[0], U_ready)
                copy(W_psum, g + 1, X[1][:], W_BANK, W_ready)
                copy(S_psum, g + 1, X[0][:], S_BANK, S_ready)
                copy(U_psum, TT * g + 2, Y[1][:], U_BANK[1], U_ready)
                for t in range(TT):
                    act.wait_ge(O_ready, TT * g + t + 1)
                    for h in range(HG):
                        z = act.activation(AT[t][:, h, :], Lm[t][:, h, :], ACT.Square, accum_out=sc[:, 8, t, h:h + 1])
                    z.then_inc(O_ssq, 1)
                act.wait_ge(o_inv, g + 1)
                act.activation(sc[:, 7], sc[:, 11], ACT.Sqrt).then_inc(o_root, 1)
                for t in range(TT):
                    act.wait_ge(g_fill, FILLS_G * g + 12 + t + 1)
                    act.activation(g_oT_hi[:, HG * g:HG * (g + 1), t * P:(t + 1) * P],
                                   bank[4 + t][:].rearrange("p (h n) -> p h n", h=HG),
                                   ACT.Copy).then_inc(o_hi_ready, 1)
            for d in range(OUT_UNITS - 1):
                split_hi(U_GDN_OUT + d + RING)
            act.wait_ge(unit_done, U_FFN[3])
            act.dma_start(final_w[:], final_norm.rearrange("(o n) -> o n", o=1).broadcast_to([P, D])
                          ).then_inc(final_loaded, 16)
            ffn(3)
            for t in range(TT):
                act.wait_ge(resid_ready, 4 * 5 + 2 * t + 2)
                square(6, t, x_sb[:, t, :], y_sb[:, t, :])
                root(RSTD_FINAL + t + 1, slice(t, t + 1))

        @block.vector
        def _(dve):
            steps = [0]

            def after(ins):
                steps[0] += 1
                ins.then_inc(vec_step, 1)
                dve.wait_ge(vec_step, steps[0])

            def split_lo(u0, i=0):
                dve.wait_ge(hi_ready, u0 + 1 + 4 * i)
                dve.tensor_tensor(w_lo[u0 % RING][:], w_raw[u0 % RING][:], w_hi[u0 % RING][:].bitcast(F32),
                                  ALU.subtract).then_inc(split_ready, 1)

            def residual(o, t, factor):
                if t == 0:
                    dve.wait_ge(acc0_done, o + 1)
                else:
                    dve.wait_ge(unit_done, RESIDUAL_UNIT[o])
                for half in range(2):
                    dve.scalar_tensor_tensor(x_sb[:, t, half * BANK:(half + 1) * BANK], bank[ACC[t][half]][:],
                                             factor, x_sb[:, t, half * BANK:(half + 1) * BANK],
                                             ALU.mult, ALU.add).then_inc(resid_ready, 1)

            def enter_lo(e, t):
                for half in range(2):
                    dve.wait_ge(xT_hi_ready, 4 * e + 2 * t + half + 1)
                    for j in range(4):
                        kt = 4 * half + j
                        z = dve.scalar_tensor_tensor(
                            xT_lo[:, kt, t * P:(t + 1) * P], bank[ENTER_BANKS[t] + half][:, j * P:(j + 1) * P],
                            norm_cols[:, e * KT + kt:e * KT + kt + 1],
                            xT_hi[:, kt, t * P:(t + 1) * P].bitcast(F32), ALU.mult, ALU.subtract)
                    z.then_inc(xT_lo_ready, 1)

            def inverse_rms(count, cols=slice(0, TT)):
                dve.wait_ge(ssq_ready, count)
                after(dve.tensor_scalar(mean_sq[:, cols], ssq[:, cols], 1.0 / D, EPS, ALU.mult, ALU.add))
                dve.reciprocal(inv_ms[:, cols], mean_sq[:, cols]).then_inc(inv_ready, 1)

            def hT_lo_part(f, j, i):
                dve.wait_ge(hT_hi_ready, NCH * f + j + 1 + 2 * i)
                at = bass.ds((j + 2 * i) * BANK, BANK)
                dve.tensor_tensor(hT_lo[:, at], bank[4 + j % 2][:], hT_hi[:, at].bitcast(F32),
                                  ALU.subtract).then_inc(hT_lo_ready, 1)

            def gate_chunk(f, j, i, before):
                u, c = U_FFN[f] + 2 * j, NCH * f + j
                for t in range(TT):
                    dve.wait_ge(silu_ready, 2 * c + t + 1 + 4 * i)
                    if t == 0 and (c >= 2 or looped(i)):
                        dve.wait_ge(hT_psum, c - 1 + 2 * i)
                    dve.scalar_tensor_tensor(h_row[j % 2][:, t, :], bank[gu_banks(j)[t]][:, FC:2 * FC],
                                             rstd[:, t:t + 1], silu_g[j % 2][:, t, :],
                                             ALU.mult, ALU.mult).then_inc(h_ready, 1)
                split_lo(u + 4, i)
                if before:
                    hT_lo_part(f, j - 1, i)
                split_lo(u + 5, i)

            def enter(e, factor, scaled=False):
                for t in range(TT):
                    if e:
                        residual(e - 1, t, factor)
                    if scaled:
                        inverse_rms(TT * e + t + 1, slice(t, t + 1))
                        dve.wait_ge(rstd_ready, RSTD_GDN + t + 1)
                        for half in range(2):
                            at = slice(half * BANK, (half + 1) * BANK)
                            dve.tensor_scalar(xs[:, t, at], x_sb[:, t, at], rstd[:, t:t + 1], None,
                                              ALU.mult).then_inc(xs_ready, 1)
                    else:
                        enter_lo(e, t)
                if scaled:
                    for t in range(TT):
                        enter_lo(e, t)
                if not scaled:
                    inverse_rms(TT * (e + 1))

            def ffn(f, factor):
                u = U_FFN[f]
                enter(E_FFN[f], factor)
                if f:
                    split_lo(u + RING - 1)
                else:
                    for n in range(1, RING):
                        split_lo(n)
                dve.wait_ge(rstd_ready, RSTD_FFN[f])
                gate_chunk(f, 0, 0, False)

                def two_chunks(i):
                    gate_chunk(f, 1, i, True)
                    gate_chunk(f, 2, i, True)

                rounds(dve, f, two_chunks)
                for d in range(DOWN_UNITS - 1):
                    if u + GU_UNITS + d + RING < U_END:
                        split_lo(u + GU_UNITS + d + RING)
                    if d == 0:
                        hT_lo_part(f, NCH - 1, 0)

            dve.wait_ge(cols_ready, 1)
            split_lo(0)
            ffn(0, None)

            enter(E_ATT, 0.5)
            split_lo(U_ATT + RING - 1)
            dve.wait_ge(a_loaded, 16 * A_LOADS)
            dve.tensor_scalar(nsink[:], sink[:], -1.0, None, ALU.mult)
            for r in range(ROT):
                dve.memset(invf[:, :, r:r + 1], float(INV_FREQ[r]))
            after(dve.tensor_copy(pos_f[:], pos_i[:]))
            for t in range(TT):
                z = dve.tensor_scalar(ang[:, 0, t, :], invf[:].rearrange("p h r -> p (h r)"), pos_f[:, t:t + 1],
                                      None, ALU.mult)
            after(z)
            after(dve.tensor_scalar(ang[:, 1], ang[:, 0], 0.0, None, ALU.add))
            dve.tensor_scalar(turns[:, 0], ang[:, 0], 1.0 / TWO_PI, None, ALU.mult)
            after(dve.tensor_scalar(turns[:, 1], ang[:, 1], 1.0 / TWO_PI, 0.25, ALU.mult, ALU.add))
            after(dve.tensor_scalar(turns[:], turns[:], ROUND, None, ALU.add))
            after(dve.tensor_scalar(turns[:], turns[:], ROUND, None, ALU.subtract))
            for part in TURN:
                after(dve.scalar_tensor_tensor(ang[:], turns[:], -part, ang[:], ALU.mult, ALU.add))
            after(dve.tensor_scalar(ang[:, 1], ang[:, 1], TWO_PI / 4, None, ALU.add))
            dve.tensor_scalar(ang[:], ang[:], PI_BELOW, -PI_BELOW, ALU.min, ALU.max).then_inc(angle_ready, 1)

            dve.wait_ge(unit_done, U_ATT + 2)
            dve.wait_ge(a_zero, 1)
            dve.wait_ge(rstd_ready, RSTD_ATT)
            for t in range(TT):
                for dst, col, signal in ((k_pad, 0, k_row), (v_pad, HKV * DH, v_row)):
                    dve.scalar_tensor_tensor(
                        dst[t][:, :, 0, 0:DH], bank[ATT_BANKS[0][t]][:, col:col + HKV * DH].rearrange(
                            "p (h d) -> p h d", d=DH), rstd[:, t:t + 1],
                        b_in[:, D + col:D + col + HKV * DH].rearrange("p (h d) -> p h d", d=DH),
                        ALU.mult, ALU.add).then_inc(signal, 1)
            split_lo(U_ATT + 4)
            split_lo(U_ATT + 5)
            for c in range(2):
                dve.wait_ge(unit_done, U_ATT + 4 + 2 * c)
                for t in range(TT):
                    dve.scalar_tensor_tensor(q_row[:, c, t, :], bank[ATT_BANKS[1 + c][t]][:], rstd[:, t:t + 1],
                                             b_in[:, c * BANK:(c + 1) * BANK], ALU.mult,
                                             ALU.add).then_inc(q_biased, 1)
                split_lo(U_ATT + 6 + 2 * c)
                split_lo(U_ATT + 7 + 2 * c)

            dve.wait_ge(a_mask, 1)
            for s in range(len(ITEMS) + 1):
                if s < len(ITEMS):
                    t, p = ITEMS[s]
                    keys = (t + 1) * P
                    pr = prob[s % 3][:, :, 0:keys]
                    mask = score_mask[:, 1, :] if t == 0 else score_mask[:].rearrange("p b k -> p (b k)")
                    dve.wait_ge(score_done, s + 1)
                    if s >= 3:
                        dve.wait_ge(a_fill, 8 + ITEM_FILL[s - 3] + 1)
                    dve.scalar_tensor_tensor(pr, bank[6 + s % 2][:, 0:2 * keys].rearrange("p (h k) -> p h k", h=2),
                                             DH ** -0.5, mask.unsqueeze(1).broadcast_to([P, 2, keys]),
                                             ALU.mult, ALU.add).then_inc(score_read, 1)
                    dve.wait_ge(score_read, s + 1)
                    after(dve.tensor_reduce(sm_max[:, s, :], pr, AX, ALU.max))
                    after(dve.scalar_tensor_tensor(sm_nmax[:, s, :], sm_max[:, s, :], -1.0,
                                                   nsink[:, 2 * p:2 * p + 2], ALU.mult, ALU.min))
                    dve.tensor_tensor(sm_off[:, s, :], sink[:, 2 * p:2 * p + 2], sm_nmax[:, s, :],
                                      ALU.add).then_inc(max_ready, 1)
                if s:
                    i = s - 1
                    t, p = ITEMS[i]
                    keys = (t + 1) * P
                    dve.wait_ge(exp_done, i + 1)
                    after(dve.tensor_tensor(sm_total[:, i, :], sm_sum[:, i, :], sm_sink[:, i, :], ALU.add))
                    after(dve.reciprocal(sm_inv[:, i, :], sm_total[:, i, :]))
                    for h in range(2):
                        z = dve.tensor_scalar(prob[i % 3][:, h, 0:keys], prob[i % 3][:, h, 0:keys],
                                              sm_inv[:, i, h:h + 1], None, ALU.mult)
                    z.then_inc(prob_ready, 1)
            for t in range(TT):
                for half in range(2):
                    dve.wait_ge(o_hi_ready, 2 * t + half + 1)
                    dst = slice(t * P, (t + 1) * P)
                    dve.tensor_tensor(a_oT_lo[:, 4 * half:4 * half + 4, dst],
                                      bank[2 * t + half][:].rearrange("p (k n) -> p k n", k=4),
                                      a_oT_hi[:, 4 * half:4 * half + 4, dst].bitcast(F32),
                                      ALU.subtract).then_inc(o_lo_ready, 1)
            for d in range(OUT_UNITS - 1):
                split_lo(U_ATT_OUT + d + RING)
            dve.wait_ge(bias_added, TT)
            ffn(1, 1.0)
            ffn(2, 0.5)

            enter(E_GDN, 0.5, scaled=True)
            split_lo(U_GDN + RING - 1)
            dve.wait_ge(wba_hi_ready, 1)
            dve.tensor_tensor(wba_lo[:, :, 0:2 * GH], wba[:], wba_hi[:, :, 0:2 * GH].bitcast(F32),
                              ALU.subtract).then_inc(wba_ready, 1)

            def conv(g, part):
                n = 4 * g + part
                for shift in range(1, CONV):
                    for h in range(HG):
                        if shift == 1 and h % 2 == 0:
                            dve.wait_ge(conv_first, 2 * (3 * g + part) + h // 2 + 1)
                        col = (CONV - 1 - shift) * 24 + part * 8 + HG * g + h
                        src = bank[CONV_BANKS[part][h // 2]]
                        z = dve.scalar_tensor_tensor(
                            cT[part][:, h, shift:SEQ], src[:, (h % 2) * SEQ:(h % 2 + 1) * SEQ - shift],
                            conv_cols[:, col:col + 1], cT[part][:, h, shift:SEQ], ALU.mult, ALU.add)
                        if shift == CONV - 1:
                            z.then_inc(conv_sum, 1)
                        elif h == HG - 1:
                            after(z)
                split_lo(U_GDN + 2 * n + 4)
                split_lo(U_GDN + 2 * n + 5)

            def gate(ins):
                gsteps[0] += 1
                ins.then_inc(gate_dve, 1)
                return gsteps[0]

            gsteps = [0]
            for g in range(NG):
                hs = slice(HG * g, HG * (g + 1))
                conv(g, 0)
                if g == 0:
                    dve.wait_ge(dec_psum, 1)
                    dve.wait_ge(g_loaded, 16 * G_LOADS)
                    ba = bank[7][:, 0:TT * P].rearrange("p (t c) -> p t c", t=TT)
                    gate(dve.tensor_tensor(gates[:, 5], ba[:, :, GH:2 * GH],
                                           head_vec[:, 1, :].unsqueeze(1).broadcast_to([P, TT, GH]), ALU.add))
                    dve.wait_ge(gate_dve, gate(dve.tensor_copy(gates[:, 0], ba[:, :, 0:GH])))
                    gate(dve.scalar_tensor_tensor(gates[:, 6], gates[:, 5], -1.0, gates[:, 5], ALU.mult, ALU.min))
                    dve.wait_ge(gate_act, 4)
                    dve.wait_ge(gate_dve, gate(dve.tensor_scalar(gates[:, 7], gates[:, 7], 1.0, None, ALU.add)))
                    gate(dve.reciprocal(gates[:, 0], gates[:, 7]))
                    dve.wait_ge(gate_dve, gate(dve.scalar_tensor_tensor(
                        gates[:, 6], gates[:, 5], 0.0, gates[:, 9], ALU.max, ALU.add)))
                    assert gate(dve.scalar_tensor_tensor(
                        gates[:, 1], gates[:, 6], -1.0, head_vec[:, 2, :].unsqueeze(1).broadcast_to([P, TT, GH]),
                        ALU.mult, ALU.mult)) == GATE_G
                    dve.wait_ge(dec_psum, 2)
                    sums = bank[6][:, 0:2 * TT * GH].rearrange("p (s t h) -> p s t h", s=2, t=TT)
                    dve.wait_ge(gate_dve, gate(dve.tensor_copy(gates[:, 2], sums[:, 0])))
                    gate(dve.tensor_tensor(gates[:, 5], sums[:, 1], gates[:, 2], ALU.subtract))
                    dve.wait_ge(gate_act, 6)
                conv(g, 1)
                conv(g, 2)
                dve.wait_ge(g_evac_act, 8 * g + 2)
                dve.wait_ge(kq_ssq, TT * (g + 1))
                dve.tensor_scalar(sc[:, 2], sc[:, 0], float(DK), float(DK) * EPS, ALU.mult, ALU.add)
                after(dve.tensor_scalar(sc[:, 3], sc[:, 1], EPS, None, ALU.add))
                dve.reciprocal(sc[:, 2:4], sc[:, 2:4]).then_inc(kq_inv, 1)
                dve.wait_ge(kq_root, g + 1)
                after(dve.tensor_tensor(sc[:, 4], sc[:, RK], gates[:, 0, :, hs], ALU.mult))
                after(dve.tensor_tensor(sc[:, 5], sc[:, 4], sc[:, RK], ALU.mult))
                after(dve.scalar_tensor_tensor(sc[:, 6], sc[:, 5], -1.0, gates[:, 3, :, hs], ALU.mult, ALU.mult))
                for h in range(HG):
                    z = dve.tensor_scalar(k_dec[:, h, :], bank[4][:, h * DK:(h + 1) * DK],
                                          gates[:, 4, 0, HG * g + h:HG * g + h + 1], None, ALU.mult)
                z.then_inc(g_evac_vec, 1)
                for h in range(HG):
                    z = dve.tensor_scalar(k_w[:, h, :], bank[5][:, h * DK:(h + 1) * DK],
                                          sc[:, 6, 1, h:h + 1], None, ALU.mult)
                z.then_inc(g_evac_vec, 1)
                for t in range(TT):
                    dve.wait_ge(g_fill, FILLS_G * g + 4 + t + 1)
                    for h in range(HG):
                        z = dve.tensor_scalar(v_beta[:, t, h, :], bank[4 + t][:, h * DK:(h + 1) * DK],
                                              sc[:, 4, t, h:h + 1], None, ALU.mult)
                    z.then_inc(g_evac_vec, 1)
                split_lo(U_GDN + 8 * g + 10)
                split_lo(U_GDN + 8 * g + 11)
                for t in range(TT):
                    dve.wait_ge(R_psum, TT * g + t + 1)
                    for h in range(HG):
                        z = dve.tensor_scalar(Lm[t][:, h, :], bank[R_BANK[t]][:, h * P:(h + 1) * P],
                                              gates[:, 2, t, HG * g + h:HG * g + h + 1], 0.0,
                                              ALU.subtract, ALU.max)
                    z.then_inc(decay_diff, 1)
                for t in range(TT):
                    dve.wait_ge(L_ready, TT * g + t + 1)
                    dve.wait_ge(KK_psum, TT * g + t + 1)
                    for h in range(HG):
                        z = dve.scalar_tensor_tensor(Y[t][:, h, :], bank[KK_BANK[t]][:, h * P:(h + 1) * P],
                                                     sc[:, 5, t, h:h + 1], Lm[t][:, h, :], ALU.mult, ALU.mult)
                    z.then_inc(A_ready, 1)
                for t in range(TT):
                    dve.wait_ge(A_ready, TT * g + t + 1)
                    after(dve.tensor_tensor(X[t][:], Y[t][:], level[1][:].unsqueeze(1).broadcast_to([P, HG, P]),
                                            ALU.mult))
                    dve.scalar_tensor_tensor(X[t][:], X[t][:], -1.0,
                                             ident[:].unsqueeze(1).broadcast_to([P, HG, P]),
                                             ALU.mult, ALU.add).then_inc(X_ready, 1)
                for t in range(TT):
                    dve.wait_ge(QK_psum, TT * g + t + 1)
                    dve.tensor_tensor(Lm[t][:].rearrange("p h n -> p (h n)"), bank[QK_BANK[t]][:],
                                      Lm[t][:].rearrange("p h n -> p (h n)"), ALU.mult).then_inc(Aqk_ready, 1)
                nl = len(LEVELS)
                for n, b in enumerate(LEVELS):
                    for t in range(TT):
                        dve.wait_ge(Y_psum, TT * (nl * g + n) + t + 1)
                        dve.tensor_tensor(Y[t][:], bank[Y_BANK[t]][:].rearrange("p (h n) -> p h n", h=HG),
                                          level[b][:].unsqueeze(1).broadcast_to([P, HG, P]),
                                          ALU.mult).then_inc(Y_ready, 1)
                    for t in range(TT):
                        if n < nl - 1:
                            dve.wait_ge(Z_psum, TT * ((nl - 1) * g + n) + t + 1)
                            dve.tensor_tensor(X[t][:].rearrange("p h n -> p (h n)"),
                                              X[t][:].rearrange("p h n -> p (h n)"), bank[Z_BANK[t]][:],
                                              ALU.subtract).then_inc(X_ready, 1)
                        dve.wait_ge(ZT_psum, TT * (nl * g + n) + t + 1)
                        dve.tensor_tensor(XT[t][:].rearrange("p h n -> p (h n)"),
                                          XT[t][:].rearrange("p h n -> p (h n)"), bank[ZT_BANK[t]][:],
                                          ALU.subtract).then_inc(XT_ready, 1)
                dve.wait_ge(O_psum, TT * g + 1)
                dve.tensor_copy(Lm[0][:].rearrange("p h n -> p (h n)"), bank[O_BANK[0]][:]).then_inc(O_ready, 1)
                dve.wait_ge(QS_psum, g + 1)
                for h in range(HG):
                    z = dve.tensor_scalar(Lm[1][:, h, :], bank[QS_BANK][:, h * P:(h + 1) * P],
                                          gates[:, 3, 1, HG * g + h:HG * g + h + 1], None, ALU.mult)
                z.then_inc(QS_ready, 1)
                dve.wait_ge(QS_ready, g + 1)
                dve.wait_ge(O_psum, TT * g + 2)
                dve.tensor_tensor(Lm[1][:].rearrange("p h n -> p (h n)"),
                                  Lm[1][:].rearrange("p h n -> p (h n)"), bank[O_BANK[1]][:],
                                  ALU.add).then_inc(O_ready, 1)
                after(dve.tensor_tensor(sc[:, 9], sc[:, RHO], sc[:, RHO], ALU.mult))
                dve.wait_ge(O_ssq, TT * (g + 1))
                after(dve.scalar_tensor_tensor(sc[:, 10], sc[:, 8], 1.0 / DK, sc[:, 9], ALU.mult, ALU.mult))
                after(dve.tensor_scalar(sc[:, 10], sc[:, 10], EPS, None, ALU.add))
                dve.reciprocal(sc[:, 11], sc[:, 10]).then_inc(o_inv, 1)
                dve.wait_ge(o_root, g + 1)
                after(dve.tensor_tensor(sc[:, 10], sc[:, 7], sc[:, RHO], ALU.mult))
                for t in range(TT):
                    dve.wait_ge(z_ready, TT * g + t + 1)
                    for h in range(HG):
                        z = dve.scalar_tensor_tensor(Lm[t][:, h, :], Lm[t][:, h, :], sc[:, 10, t, h:h + 1],
                                                     z_gate[:, t, h, :], ALU.mult, ALU.mult)
                    z.then_inc(O_final, 1)
                for t in range(TT):
                    dve.wait_ge(o_hi_ready, 4 + TT * g + t + 1)
                    dst = slice(t * P, (t + 1) * P)
                    dve.tensor_tensor(g_oT_lo[:, HG * g:HG * (g + 1), dst],
                                      bank[4 + t][:].rearrange("p (h n) -> p h n", h=HG),
                                      g_oT_hi[:, HG * g:HG * (g + 1), dst].bitcast(F32),
                                      ALU.subtract).then_inc(o_lo_ready, 1)
            for d in range(OUT_UNITS - 1):
                split_lo(U_GDN_OUT + d + RING)
            ffn(3, 1.0)

            for t in range(TT):
                residual(5, t, 0.5)
            dve.wait_ge(final_loaded, 16)
            for t in range(TT):
                inverse_rms(TT * 6 + t + 1, slice(t, t + 1))
                dve.wait_ge(rstd_ready, RSTD_FINAL + t + 1)
                dve.scalar_tensor_tensor(y_sb[:, t, :], x_sb[:, t, :], rstd[:, t:t + 1], final_w[:],
                                         ALU.mult, ALU.mult).then_inc(y_ready, 1)

        @block.tensor
        def _(pe):
            def products(out_ap, a, b, start, stop, **kw):
                pe.matmul(out_ap, a[0], b[0], start=start, stop=False, **kw)
                pe.matmul(out_ap, a[0], b[1], start=False, stop=False, **kw)
                return pe.matmul(out_ap, a[1], b[0], start=False, stop=stop, **kw)

            def xT(kt, t):
                at = slice(t * P, (t + 1) * P)
                return xT_hi[:, kt, at], xT_lo[:, kt, at]

            def ring(u0, at):
                return w_hi[u0 % RING][:, at], w_lo[u0 % RING][:, at]

            def enter(e, t):
                src = xs if e == E_GDN else x_sb
                for half in range(2):
                    if e == 0:
                        pe.wait_ge(x_loaded[t], 16)
                    elif e == E_GDN:
                        pe.wait_ge(xs_ready, 2 * t + half + 1)
                    else:
                        pe.wait_ge(resid_ready, 4 * (e - 1) + 2 * t + half + 1)
                    for j in range(4):
                        kt = 4 * half + j
                        z = pe.transpose(bank[ENTER_BANKS[t] + half][:, j * P:(j + 1) * P],
                                         src[:, t, kt * P:(kt + 1) * P], ident[:])
                    z.then_inc(xT_psum, 1)

            def in_unit(u0, i, kh, banks, e=None):
                pe.wait_ge(split_ready, u0 + 1 + 4 * i)
                for t in range(TT):
                    if e is not None:
                        pe.wait_ge(xT_lo_ready, 4 * e + 2 * t + 2)
                    for j in range(4):
                        z = products(bank[banks[t]][:], xT(4 * kh + j, t), ring(u0, slice(j * BANK, (j + 1) * BANK)),
                                     start=(kh == 0 and j == 0), stop=(kh == 1 and j == 3))
                z.then_inc(unit_done, 1)

            def gate_chunk(f, j, i):
                u, c = U_FFN[f] + 2 * j, NCH * f + j
                if j and (c >= 2 or looped(i)):
                    pe.wait_ge(h_ready, 2 * (c - 1) + 4 * i)
                for kh in range(2):
                    in_unit(u + kh, i, kh, gu_banks(j), E_FFN[f] if j == 0 and kh == 0 else None)

            def h_transposes(f, j, i):
                c = NCH * f + j
                pe.wait_ge(h_ready, 2 * c + 2 + 4 * i)
                for k in range(2):
                    for t in range(TT):
                        z = pe.transpose(bank[4 + j % 2][:, k * SEQ + t * P:k * SEQ + (t + 1) * P],
                                         h_row[j % 2][:, t, k * P:(k + 1) * P], ident[:])
                z.then_inc(hT_psum, 1)

            def out_unit(u0, d, n, operand, ready, e):
                pe.wait_ge(split_ready, u0 + d + 1)
                for t in range(TT):
                    ready(2 * d, t)
                    for j in range(2):
                        kt = 2 * d + j
                        for half in range(2):
                            z = products(bank[ACC[t][half]][:], operand(kt, t),
                                         ring(u0 + d, slice(j * D + half * BANK, j * D + (half + 1) * BANK)),
                                         start=(kt == 0), stop=(kt == 2 * n - 1))
                        if d == n - 1 and t == 1 and j == 0 and e not in (None, E_GDN):
                            enter(e, 0)
                    if d == n - 1 and t == 0:
                        z.then_inc(acc0_done, 1)
                z.then_inc(unit_done, 1)
                if d == n - 1 and e is not None:
                    if e == E_GDN:
                        enter(e, 0)
                    enter(e, 1)

            def hT(kt, t):
                at = slice(kt * SEQ + t * P, kt * SEQ + (t + 1) * P)
                return hT_hi[:, at], hT_lo[:, at]

            def ffn(f, e_next):
                gate_chunk(f, 0, 0)

                def two_chunks(i):
                    gate_chunk(f, 1, i)
                    h_transposes(f, 0, i)
                    gate_chunk(f, 2, i)
                    h_transposes(f, 1, i)

                rounds(pe, f, two_chunks)
                for d in range(DOWN_UNITS):
                    out_unit(U_FFN[f] + GU_UNITS, d, DOWN_UNITS, hT,
                             lambda kt, t: pe.wait_ge(hT_lo_ready, NCH * f + kt // 2 + 1), e_next)
                    if d == 1:
                        h_transposes(f, NCH - 1, 0)

            pe.wait_ge(ident_ready, 1)
            pe.wait_ge(rows_loaded, 16 * 7)
            pe.transpose(bank[0][:, 0:P], norm_rows[:], ident[:])
            pe.transpose(bank[0][:, P:2 * P], conv_rows[:], ident[:]).then_inc(cols_psum, 1)
            for t in range(TT):
                enter(0, t)
            ffn(0, E_ATT)

            def a_bank(f):
                if f >= 2:
                    pe.wait_ge(a_evac, f - 1)
                return bank[4 + f % 2]

            def a_fill4(f, sources):
                b = a_bank(f)
                for n, s in enumerate(sources):
                    z = pe.transpose(b[:, n * P:(n + 1) * P], s, ident[:])
                z.then_inc(a_fill, 1)

            for n in range(3):
                for kh in range(2):
                    in_unit(U_ATT + 2 * n + kh, 0, kh, ATT_BANKS[n], E_ATT if n == 0 and kh == 0 else None)
                if n == 1:
                    for t in range(TT):
                        pe.wait_ge(k_rot, t + 1)
                        for half in range(2):
                            a_fill4(2 * t + half, [k_pad[t][:, 2 * half + m // 2, m % 2, :] for m in range(4)])
            for c in range(2):
                for t in range(TT):
                    pe.wait_ge(q_rot, 2 * c + t + 1)
                    a_fill4(4 + 2 * c + t, [q_row[:, c, t, m * P:(m + 1) * P] for m in range(4)])
            pe.wait_ge(v_both, TT)
            for s in range(len(ITEMS) + 3):
                if s < len(ITEMS):
                    t, p = ITEMS[s]
                    pe.wait_ge(a_evac, 6 if p < 4 else 8)
                    if s >= 2:
                        pe.wait_ge(score_read, s - 1)
                    keys = (t + 1) * P
                    pe.matmul(bank[6 + s % 2][:, 0:2 * keys].rearrange("p (h k) -> p h k", h=2),
                              qT[:, p, t * P:(t + 1) * P], kzT[:, p // 2, :, 0:keys],
                              start=True, stop=True).then_inc(score_done, 1)
                for n, (t, items) in enumerate(FILLS):
                    if items[-1] == s - 2:
                        pe.wait_ge(prob_ready, items[-1] + 1)
                        if t == 0:
                            a_fill4(8 + n, [prob[i % 3][:, h, 0:P] for h in range(2) for i in items])
                        else:
                            a_fill4(8 + n, [prob[items[0] % 3][:, h, b * P:(b + 1) * P]
                                            for h in range(2) for b in range(2)])
                    if items[-1] == s - 3:
                        pe.wait_ge(a_evac, 8 + n + 1)
                        pT = probT[n % 2]
                        if t == 0:
                            kv, at = n, slice((n % 2) * 2 * P, (n % 2) * 2 * P + 2 * P)
                            o = bank[n // 2][:, at]
                            pe.matmul(o, v_pad[0][:, kv, 0, :], pT[:, 0:2 * P], start=True, stop=False)
                            z = pe.matmul(o, v_pad[0][:, kv, 1, :], pT[:, 2 * P:4 * P], start=False, stop=True)
                        else:
                            p = n - HKV
                            o = bank[2 + p // 4][:, (p % 4) * P:(p % 4 + 1) * P]
                            for m in range(4):
                                h, b = m // 2, m % 2
                                z = pe.matmul(o, v_pad[b][:, p // 2, h, :], pT[:, m * P:(m + 1) * P],
                                              start=(m == 0), stop=(m == 3))
                        z.then_inc(pv_done, 1)

            def att_o(kt, t):
                at = slice(t * P, (t + 1) * P)
                return a_oT_hi[:, kt, at], a_oT_lo[:, kt, at]

            for d in range(OUT_UNITS):
                out_unit(U_ATT_OUT, d, OUT_UNITS, att_o,
                         lambda kt, t: pe.wait_ge(o_lo_ready, 4), E_FFN[1])
            ffn(1, E_FFN[2])
            ffn(2, E_GDN)

            def g_transposes(g, f, source):
                t = f % 2
                if f < 2:
                    if g:
                        pe.wait_ge(o_lo_ready, 4 + TT * (g - 1) + t + 1)
                elif f < 4:
                    pe.wait_ge(g_evac_act, 8 * g + t + 1)
                elif f < 8:
                    pe.wait_ge(g_evac_vec, 4 * g + (f - 4) + 1)
                else:
                    pe.wait_ge(g_evac_act, 8 * g + 2 + (f - 8) + 1)
                for h in range(HG):
                    z = pe.transpose(bank[4 + t][:, h * P:(h + 1) * P], source(t, h), ident[:])
                z.then_inc(g_fill, 1)

            def channel_unit(u0, kh, banks, e=None):
                pe.wait_ge(split_ready, u0 + 1)
                if e is not None:
                    pe.wait_ge(xT_lo_ready, 4 * e + 4)
                for h in range(HG):
                    for j in range(4):
                        kt = 4 * kh + j
                        z = products(bank[banks[h // 2]][:, (h % 2) * SEQ:(h % 2 + 1) * SEQ],
                                     ring(u0, slice(j * BANK + h * P, j * BANK + (h + 1) * P)),
                                     (xT_hi[:, kt, :], xT_lo[:, kt, :]),
                                     start=(kt == 0 and h % 2 == 0), stop=(kt == KT - 1),
                                     skip_group_check=True)
                z.then_inc(unit_done, 1)

            def heads(b, a, m, ready=None):
                for h in range(HG):
                    z = pe.matmul(bank[b][:, h * P:(h + 1) * P], a(h), m(h), start=True, stop=True)
                return z

            q_T, k_T, v_T = cT
            nl = len(LEVELS)
            for g in range(NG):
                u = U_GDN + 8 * g
                tile = [slice(t * P, (t + 1) * P) for t in range(TT)]
                if g:
                    pe.wait_ge(O_ready, TT * g)
                for kh in range(2):
                    channel_unit(u + kh, kh, CONV_BANKS[0], E_GDN if g == 0 and kh == 0 else None)
                if g == 0:
                    pe.wait_ge(wba_ready, 1)
                    for kt in range(KT):
                        z = products(bank[6][:, 0:SEQ], (wba_hi[:, kt, :], wba_lo[:, kt, :]),
                                     (xT_hi[:, kt, :], xT_lo[:, kt, :]), start=(kt == 0), stop=(kt == KT - 1))
                    z.then_inc(ba_psum, 1)
                channel_unit(u + 2, 0, CONV_BANKS[1])
                if g == 0:
                    pe.wait_ge(ba_ready, 1)
                    for t in range(TT):
                        z = pe.transpose(bank[7][:, tile[t]], ba_T[:, tile[t]], ident[:])
                    z.then_inc(dec_psum, 1)
                channel_unit(u + 3, 1, CONV_BANKS[1])
                if g == 0:
                    pe.wait_ge(gate_dve, GATE_G)
                    pe.wait_ge(g_masks, 1)
                    n = TT * GH
                    pe.matmul(bank[6][:, 0:n], upper[:], gates[:, 1].rearrange("p t h -> p (t h)"),
                              start=True, stop=True)
                    pe.matmul(bank[6][:, n:2 * n], ones[:], gates[:, 1].rearrange("p t h -> p (t h)"),
                              start=True, stop=True).then_inc(dec_psum, 1)
                pe.wait_ge(conv_ready, 3 * g + 1)
                for t in range(TT):
                    g_transposes(g, t, lambda t, h: q_T[:, h, tile[t]])
                if g == 0:
                    pe.wait_ge(gate_dve, GATE_G + 2)
                for kh in range(2):
                    channel_unit(u + 4 + kh, kh, CONV_BANKS[2])
                pe.wait_ge(conv_ready, 3 * g + 2)
                for t in range(TT):
                    g_transposes(g, 2 + t, lambda t, h: k_T[:, h, tile[t]])
                for kh in range(2):
                    in_unit(u + 6 + kh, 0, kh, (0, 1))
                pe.wait_ge(conv_ready, 3 * g + 3)
                for t in range(TT):
                    g_transposes(g, 4 + t, lambda t, h: v_T[:, h, tile[t]])
                for t in range(TT):
                    pe.wait_ge(gU_ready, TT * g + t + 1)
                    pe.matmul(bank[R_BANK[t]][:], ones[:], gU[:, t].rearrange("p h n -> p (h n)"),
                              start=True, stop=True).then_inc(R_psum, 1)
                pe.wait_ge(z_silu, TT * (g + 1))
                for t in range(TT):
                    heads(KK_BANK[t], lambda h: k_T[:, h, tile[t]],
                          lambda h: k_T[:, h, tile[t]]).then_inc(KK_psum, 1)
                    heads(QK_BANK[t], lambda h: q_T[:, h, tile[t]],
                          lambda h: k_T[:, h, tile[t]]).then_inc(QK_psum, 1)
                for t in range(TT):
                    pe.wait_ge(A_ready, TT * g + t + 1)
                    g_transposes(g, 6 + t, lambda t, h: Y[t][:, h, :])
                for t in range(TT):
                    pe.wait_ge(X_ready, 2 * nl * g + t + 1)
                    g_transposes(g, 8 + t, lambda t, h: X[t][:, h, :])
                for t in range(TT):
                    pe.wait_ge(Aqk_ready, TT * g + t + 1)
                    g_transposes(g, 10 + t, lambda t, h: Lm[t][:, h, :])
                for n, b in enumerate(LEVELS):
                    for t in range(TT):
                        pe.wait_ge(X_ready, 2 * nl * g + 2 * n + t + 1)
                        heads(Y_BANK[t], lambda h: AT[t][:, h, :],
                              lambda h: X[t][:, h, :]).then_inc(Y_psum, 1)
                    for t in range(TT):
                        if n == 0:
                            pe.wait_ge(g_evac_act, 8 * g + 4 + t + 1)
                        else:
                            pe.wait_ge(XT_ready, 2 * nl * g + 2 * (n - 1) + t + 1)
                        pe.wait_ge(Y_ready, 2 * nl * g + 2 * n + t + 1)
                        if n < nl - 1:
                            heads(Z_BANK[t], lambda h: XT[t][:, h, :],
                                  lambda h: Y[t][:, h, :]).then_inc(Z_psum, 1)
                        heads(ZT_BANK[t], lambda h: Y[t][:, h, :],
                              lambda h: XT[t][:, h, :]).then_inc(ZT_psum, 1)
                pe.wait_ge(XT_ready, 2 * nl * (g + 1) - 1)
                heads(U_BANK[0], lambda h: XT[0][:, h, :], lambda h: v_beta[:, 0, h, :]).then_inc(U_psum, 1)
                pe.wait_ge(XT_ready, 2 * nl * (g + 1))
                heads(W_BANK, lambda h: k_w[:, h, :], lambda h: XT[1][:, h, :]).then_inc(W_psum, 1)
                pe.wait_ge(U_ready, TT * g + 1)
                heads(S_BANK, lambda h: k_dec[:, h, :], lambda h: Y[0][:, h, :]).then_inc(S_psum, 1)
                pe.wait_ge(g_evac_act, 8 * g + 8)
                heads(O_BANK[0], lambda h: AqkT[0][:, h, :], lambda h: Y[0][:, h, :]).then_inc(O_psum, 1)
                pe.wait_ge(W_ready, g + 1)
                pe.wait_ge(S_ready, g + 1)
                for h in range(HG):
                    o = bank[U_BANK[1]][:, h * P:(h + 1) * P]
                    pe.matmul(o, XT[1][:, h, :], v_beta[:, 1, h, :], start=True, stop=False)
                    z = pe.matmul(o, X[1][:, h, :], X[0][:, h, :], start=False, stop=True)
                z.then_inc(U_psum, 1)
                heads(QS_BANK, lambda h: q_T[:, h, tile[1]], lambda h: X[0][:, h, :]).then_inc(QS_psum, 1)
                pe.wait_ge(U_ready, TT * g + 2)
                heads(O_BANK[1], lambda h: AqkT[1][:, h, :], lambda h: Y[1][:, h, :]).then_inc(O_psum, 1)
                for t in range(TT):
                    pe.wait_ge(O_final, TT * g + t + 1)
                    g_transposes(g, 12 + t, lambda t, h: Lm[t][:, h, :])

            def gdn_o(kt, t):
                at = slice(t * P, (t + 1) * P)
                return g_oT_hi[:, kt, at], g_oT_lo[:, kt, at]

            for d in range(OUT_UNITS):
                out_unit(U_GDN_OUT, d, OUT_UNITS, gdn_o,
                         lambda kt, t: pe.wait_ge(o_lo_ready, 4 + TT * (kt // HG) + t + 1), E_FFN[3])
            ffn(3, None)

_INS = ["x", "positions", "ffn1_norm", "ffn1_w_gate_up", "ffn1_w_down", "mix_norm", "ffn2_norm",
        "ffn2_w_gate_up", "ffn2_w_down", "attn_w_in", "attn_b_in", "attn_sinks", "attn_w_out",
        "attn_b_out", "gdn_w_in", "gdn_conv_w", "gdn_A_log", "gdn_dt_bias", "gdn_norm_w",
        "gdn_w_out", "final_norm"]
_OUT = (1, SEQ, D)


def kernel(**inputs):
    import concourse.bacc as _bacc
    from concourse.bass_utils import run_bass_kernel_spmd as _run

    nc = _bacc.Bacc("TRN2", target_bir_lowering=False, num_devices=1)
    arrays, args = {}, []
    for name in _INS:
        a = np.ascontiguousarray(inputs[name])
        arrays[f"in_{name}"] = a
        args.append(nc.dram_tensor(f"in_{name}", a.shape, mybir.dt.from_np(a.dtype), kind="ExternalInput").ap())
    args.append(nc.dram_tensor("out_0", _OUT, F32, kind="ExternalOutput").ap())
    build(nc, *args)
    r = _run(nc, [arrays], core_ids=[0])
    return r.results[0]["out_0"]
```

```python
from contextlib import ExitStack

import numpy as np

import concourse.bass as bass
from concourse import mybir

ALU = mybir.AluOpType
ACT = mybir.ActivationFunctionType
F32 = mybir.dt.float32
F32R = mybir.dt.float32r
BF16 = mybir.dt.bfloat16
I32 = mybir.dt.int32
AX = mybir.AxisListType.X

P = 128
D = 1024
SEQ = 256
TT = SEQ // P
KT = D // P
DFF = 2816
FC = 256
NCH = DFF // FC
EPS = 1e-6
BANK = 512
UNIT = 2048
RING = 4

HQ, HKV, DH = 16, 4, 64
PAIRS = HQ // 2
ROT = 8
THETA = 500000.0
MASKED = -1e30

GH, DK = 8, 128
HG = 4
NG = GH // HG
CONV = 4
LEVELS = [2, 4, 8, 16, 32, 64]

GU_UNITS = 2 * NCH
DOWN_UNITS = DFF // (2 * P)
FFN_UNITS = GU_UNITS + DOWN_UNITS
ATT_IN_UNITS, OUT_UNITS = 6, D // (2 * P)
GDN_IN_UNITS = 4 * NG * 2

U_FFN = [0] * 4
U_FFN[0] = 0
U_ATT = U_FFN[0] + FFN_UNITS
U_ATT_OUT = U_ATT + ATT_IN_UNITS
U_FFN[1] = U_ATT_OUT + OUT_UNITS
U_FFN[2] = U_FFN[1] + FFN_UNITS
U_GDN = U_FFN[2] + FFN_UNITS
U_GDN_OUT = U_GDN + GDN_IN_UNITS
U_FFN[3] = U_GDN_OUT + OUT_UNITS
U_END = U_FFN[3] + FFN_UNITS

E_FFN, E_ATT, E_GDN = [0, 2, 3, 5], 1, 4
GDN_COLS = [part * D + g * HG * DK for g in range(NG) for part in range(4)]
ATT_COLS = [D, 0, BANK]


A_LOADS = G_LOADS = 4
GATE_G = 7
NORM_ROWS, CONV_ROWS = 2 * 3 * KT, CONV * 3 * D // P


def norm_col(e, kt):
    return (e % 3) * 2 * KT + (e // 3) * KT + kt


def quarters(e):
    if e in (0, E_GDN, 6):
        return [(t, half) for t in range(TT) for half in range(2)]
    return [(t, half) for half in range(2) for t in range(TT)]


RSTD_FFN, RSTD_ATT, RSTD_GDN, RSTD_FINAL = [1, 3, 4, 7], 2, 4, 7
RESIDUAL_UNIT = [U_ATT, U_FFN[1], U_FFN[2], U_GDN, U_FFN[3], U_END]

PHASE_UNIT = [U_FFN[0], U_ATT, U_FFN[1], U_FFN[2], U_GDN, U_FFN[3]]

POOL_UNITS = [U_GDN + 5 + 2 * n for n in range(4 * NG)]


def splits(u):
    by_pool = sum(v <= u for v in POOL_UNITS)
    return by_pool if u in POOL_UNITS else u + 1 - by_pool


ATT_BANKS = [(6, 7), (0, 1), (2, 3)]
HALF_PAIRS = PAIRS // 2
ITEMS = [(t, p) for c in range(2) for t in range(TT) for p in range(c * HALF_PAIRS, (c + 1) * HALF_PAIRS)]
FILLS = [f for i in range(0, len(ITEMS), 2)
         for f in ([(i, i + 1)] if ITEMS[i][0] == 0 else [(i,), (i + 1,)])]
ITEM_FILL = [n for n, items in enumerate(FILLS) for _ in items]
STEPS = len(ITEMS) + 3
PROBS = 4
Q_BIAS_STEP, Q_STEP = 5, 7
Q_FIRST, Q_PARTS = 10, [2, 1, 1, 1, 1]
OUT_FIRST, OUT_PARTS = 12, [1] * 6 + [2]
FIRST_FILLS = 6
Q_FILL = FIRST_FILLS + sum(items[-1] + 2 <= Q_STEP for items in FILLS)
FILL_NO = [FIRST_FILLS + n + (2 if items[-1] + 2 > Q_STEP else 0) for n, items in enumerate(FILLS)]
OUTS = [(c, t) for c in range(2) for t in range(TT)]
OUT_LAST = [max(i for i, (t1, p) in enumerate(ITEMS) if t1 == t and p // HALF_PAIRS == c) for c, t in OUTS]
OUT_PV = [ITEM_FILL[i] + 1 for i in OUT_LAST]
OUT_STEP = [i + 4 for i in OUT_LAST]

CONV_BANKS = [(0, 1), (2, 3), (6, 7)]
R_BANK, KK_BANK, QK_BANK = [2, 3], [6, 2], [7, 3]
Y_BANK, Z_BANK, ZT_BANK = [2, 3], [6, 0], [7, 1]
U_BANK, O_BANK, W_BANK, S_BANK, QS_BANK = [2, 6], [7, 3], 3, 6, 2
RHO, RK = 12, 13
FILL_Q, FILL_K, FILL_A, FILL_X, FILL_AQK, FILL_V, FILL_O, FILLS_G = range(0, 16, 2)
EVACS_G = 10

TWO_PI = 2 * np.pi
TURN = [6.28125, 0.001935302734375, TWO_PI - 6.28125 - 0.001935302734375]
ROUND = 12582912.0
PI_BELOW = 3.1415925
INV_FREQ = THETA ** (-np.arange(0, 2 * ROT, 2, dtype=np.float32) / (2 * ROT))


def build(nc, x, positions, ffn1_norm, ffn1_w_gate_up, ffn1_w_down, mix_norm, ffn2_norm,
          ffn2_w_gate_up, ffn2_w_down, attn_w_in, attn_b_in, attn_sinks, attn_w_out, attn_b_out,
          gdn_w_in, gdn_conv_w, gdn_A_log, gdn_dt_bias, gdn_norm_w, gdn_w_out, final_norm, out):
    ctx = ExitStack()
    with ctx:
        def sb(name, shape, dt=F32, where=ctx):
            return where.enter_context(nc.sbuf_tensor(name, shape, dt))

        def sem(name):
            return ctx.enter_context(nc.semaphore(name))

        x_sb = sb("x_sb", [P, TT, D])
        xT_hi = sb("xT_hi", [P, KT, SEQ], F32R)
        xT_lo = sb("xT_lo", [P, KT, SEQ], F32R)
        w_raw = [sb(f"w_raw{i}", [P, UNIT]) for i in range(RING)]
        w_hi = [sb(f"w_hi{i}", [P, UNIT], F32R) for i in range(RING)]
        w_lo = [sb(f"w_lo{i}", [P, UNIT], F32R) for i in range(RING)]
        y_sb = sb("y_sb", [P, TT, D])
        ident = sb("ident", [P, P])
        norm_rows = sb("norm_rows", [NORM_ROWS, P])
        norm_cols = sb("norm_cols", [P, NORM_ROWS])
        conv_rows = sb("conv_rows", [CONV_ROWS, P])
        conv_cols = sb("conv_cols", [P, CONV_ROWS])
        ssq = sb("ssq", [P, TT])
        spare = sb("spare", [P, 1])
        diag_rstd = sb("diag_rstd", [P, TT, P])
        mean_sq = sb("mean_sq", [P, TT])
        inv_ms = sb("inv_ms", [P, TT])
        rstd = sb("rstd", [P, TT])

        with ExitStack() as ffn_mem:
            hT_hi = sb("hT_hi", [P, DFF // P * SEQ], F32R, ffn_mem)
            hT_lo = sb("hT_lo", [P, DFF // P * SEQ], F32R, ffn_mem)
            silu_g = [sb(f"silu_g{i}", [P, TT, FC], F32, ffn_mem) for i in range(2)]
            h_row = [sb(f"h_row{i}", [P, TT, FC], F32, ffn_mem) for i in range(2)]
            final_w = sb("final_w", [P, D], F32, ffn_mem)

        with ExitStack() as att_mem:
            a_oT_hi = sb("a_oT_hi", [P, KT, SEQ], F32R, att_mem)
            a_oT_lo = sb("a_oT_lo", [P, KT, SEQ], F32R, att_mem)
            b_in = sb("b_in", [P, 3 * BANK], F32, att_mem)
            b_out = sb("b_out", [P, D], F32, att_mem)
            sink = sb("sink", [P, HQ], F32, att_mem)
            nsink = sb("nsink", [P, HQ], F32, att_mem)
            k_pad = [sb(f"k_pad{t}", [P, HKV, 2, P], F32, att_mem) for t in range(TT)]
            v_pad = [sb(f"v_pad{t}", [P, HKV, 2, P], F32, att_mem) for t in range(TT)]
            kzT = sb("kzT", [P, HKV, 2, SEQ], F32, att_mem)
            qT = sb("qT", [P, PAIRS, SEQ], F32, att_mem)
            score_mask = sb("score_mask", [P, 2, P], BF16, att_mem)
            ident_bf = sb("ident_bf", [P, P], BF16, att_mem)
            prob = [sb(f"prob{i}", [P, 2, SEQ], F32, att_mem) for i in range(PROBS)]
            probT = [sb(f"probT{i}", [P, BANK], F32, att_mem) for i in range(2)]
            sm_max = sb("sm_max", [P, TT * PAIRS, 2], F32, att_mem)
            sm_nmax = sb("sm_nmax", [P, TT * PAIRS, 2], F32, att_mem)
            sm_off = sb("sm_off", [P, TT * PAIRS, 2], F32, att_mem)
            sm_sink = sb("sm_sink", [P, TT * PAIRS, 2], F32, att_mem)
            sm_sum = sb("sm_sum", [P, TT * PAIRS, 2], F32, att_mem)
            sm_total = sb("sm_total", [P, TT * PAIRS, 2], F32, att_mem)
            sm_inv = sb("sm_inv", [P, TT * PAIRS, 2], F32, att_mem)
            pos_i = sb("pos_i", [P, TT], I32, att_mem)
            pos_f = sb("pos_f", [P, TT], F32, att_mem)
            invf = sb("invf", [P, 8, ROT], F32, att_mem)
            ang = sb("ang", [P, 2, TT, 8 * ROT], F32, att_mem)
            turns = sb("turns", [P, 2, TT, 8 * ROT], F32, att_mem)
            sincos = sb("sincos", [P, 2, TT, 8, ROT], F32, att_mem)
            rot = [sb(f"rot{i}", [P, 8, ROT], F32, att_mem) for i in range(4)]

        with ExitStack() as gdn_mem:
            g_oT_hi = sb("g_oT_hi", [P, KT, SEQ], F32R, gdn_mem)
            g_oT_lo = sb("g_oT_lo", [P, KT, SEQ], F32R, gdn_mem)
            gates = sb("gates", [P, 10, TT, GH], F32, gdn_mem)
            head_vec = sb("head_vec", [P, 3, GH], F32, gdn_mem)
            norm_w = sb("norm_w", [P, DK], F32, gdn_mem)
            cT = [sb(f"{n}_T", [P, HG, SEQ], F32, gdn_mem) for n in "qkv"]
            v_beta = sb("v_beta", [P, TT, HG, DK], F32, gdn_mem)
            k_dec = sb("k_dec", [P, HG, DK], F32, gdn_mem)
            k_w = sb("k_w", [P, HG, DK], F32, gdn_mem)
            lower = sb("lower", [P, P], F32, gdn_mem)
            upper = sb("upper", [P, P], F32, gdn_mem)
            ones = sb("ones", [P, P], F32, gdn_mem)
            level1 = sb("level1", [P, P], F32, gdn_mem)
            level = {b: sb(f"level{b}", [P, HG * P // 2], F32, gdn_mem) for b in LEVELS}
            AqkT = [sb(f"AqkT{t}", [P, HG, P], F32, gdn_mem) for t in range(TT)]
            sc = sb("sc", [P, 14, TT, HG], F32, gdn_mem)
            with ExitStack() as early:
                wba = sb("wba", [P, KT, 2 * GH], F32, early)
                wba_hi = sb("wba_hi", [P, KT, P], F32R, early)
                wba_lo = sb("wba_lo", [P, KT, P], F32R, early)
                ba_T = sb("ba_T", [P, SEQ], F32, early)
            with ExitStack() as late:
                gU = sb("gU", [P, TT, HG, P], F32, late)
                Lm = [sb(f"Lm{t}", [P, HG, P], F32, late) for t in range(TT)]
                AT = [sb(f"AT{t}", [P, HG, P], F32, late) for t in range(TT)]
                Y = [sb(f"Y{t}", [P, HG, P], F32, late) for t in range(TT)]
                X = [sb(f"X{t}", [P, HG, P], F32, late) for t in range(TT)]
                XT = [sb(f"XT{t}", [P, HG, P], F32, late) for t in range(TT)]

        bank = [ctx.enter_context(nc.psum_tensor(f"bank{i}", [P, BANK], F32)) for i in range(8)]
        ENTER_BANKS = [4, 2]
        ACC = [(6, 7), (0, 1)]
        GATE_UP = [(6, 7), (0, 1), (2, 3)]

        def gu_banks(j):
            return GATE_UP[0] if j == 0 else GATE_UP[1] if j % 2 else GATE_UP[2]

        raw_loaded = [sem(f"raw_loaded{i}") for i in range(RING)]
        first_hi = sem("first_hi")
        first_split = sem("first_split")
        hi_ready = sem("hi_ready")
        split_ready = sem("split_ready")
        pool_split = sem("pool_split")
        unit_done = sem("unit_done")
        x_loaded = [sem(f"x_loaded{t}") for t in range(TT)]
        rows_loaded = sem("rows_loaded")
        conv_loaded = sem("conv_loaded")
        ident_ready = sem("ident_ready")
        cols_psum = sem("cols_psum")
        cols_ready = sem("cols_ready")
        conv_cols_ready = sem("conv_cols_ready")
        resid_ready = sem("resid_ready")
        diag_ready = sem("diag_ready")
        xT_psum = sem("xT_psum")
        xT_hi_ready = sem("xT_hi_ready")
        xT_lo_ready = sem("xT_lo_ready")
        ssq_ready = sem("ssq_ready")
        inv_ready = sem("inv_ready")
        rstd_ready = sem("rstd_ready")
        vec_step = sem("vec_step")
        pool_step = sem("pool_step")
        acc_done = sem("acc_done")
        silu_ready = sem("silu_ready")
        h_ready = sem("h_ready")
        hT_psum = sem("hT_psum")
        hT_hi_ready = sem("hT_hi_ready")
        hT_lo_ready = sem("hT_lo_ready")
        a_loaded = sem("a_loaded")
        a_mask = sem("a_mask")
        a_zero = sem("a_zero")
        bias_added = sem("bias_added")
        angle_ready = sem("angle_ready")
        rope_ready = sem("rope_ready")
        k_row = sem("k_row")
        v_row = sem("v_row")
        q_biased = sem("q_biased")
        k_rot = sem("k_rot")
        v_both = sem("v_both")
        q_rot = sem("q_rot")
        a_fill = sem("a_fill")
        a_evac = sem("a_evac")
        score_done = sem("score_done")
        max_ready = sem("max_ready")
        exp_done = sem("exp_done")
        prob_ready = sem("prob_ready")
        pv_done = sem("pv_done")
        o_hi_ready = sem("o_hi_ready")
        o_lo_ready = sem("o_lo_ready")
        g_loaded = sem("g_loaded")
        g_masks = sem("g_masks")
        wba_zero = sem("wba_zero")
        wba_hi_ready = sem("wba_hi_ready")
        wba_ready = sem("wba_ready")
        ba_psum = sem("ba_psum")
        ba_ready = sem("ba_ready")
        gate_dve = sem("gate_dve")
        gate_act = sem("gate_act")
        dec_psum = sem("dec_psum")
        conv_first = sem("conv_first")
        conv_sum = sem("conv_sum")
        conv_ready = sem("conv_ready")
        z_silu = sem("z_silu")
        z_ready = sem("z_ready")
        g_fill = sem("g_fill")
        g_evac_act = sem("g_evac_act")
        g_evac_vec = sem("g_evac_vec")
        kq_inv = sem("kq_inv")
        kq_root = sem("kq_root")
        o_inv = sem("o_inv")
        o_root = sem("o_root")
        kq_ssq = sem("kq_ssq")
        gU_ready = sem("gU_ready")
        R_psum = sem("R_psum")
        decay_diff = sem("decay_diff")
        decay_exp = sem("decay_exp")
        L_ready = sem("L_ready")
        KK_psum = sem("KK_psum")
        QK_psum = sem("QK_psum")
        A_ready = sem("A_ready")
        Aqk_ready = sem("Aqk_ready")
        X_ready = sem("X_ready")
        XT_psum = sem("XT_psum")
        XT_copied = sem("XT_copied")
        XT_ready = sem("XT_ready")
        Y_psum = sem("Y_psum")
        Y_ready = sem("Y_ready")
        Z_psum = sem("Z_psum")
        ZT_psum = sem("ZT_psum")
        U_psum = sem("U_psum")
        U_ready = sem("U_ready")
        W_psum = sem("W_psum")
        W_ready = sem("W_ready")
        S_psum = sem("S_psum")
        S_ready = sem("S_ready")
        QS_psum = sem("QS_psum")
        QS_ready = sem("QS_ready")
        O_psum = sem("O_psum")
        O_ready = sem("O_ready")
        O_ssq = sem("O_ssq")
        O_final = sem("O_final")
        final_loaded = sem("final_loaded")
        y_ready = sem("y_ready")
        out_stored = sem("out_stored")
        def rounds(eng, f, body):
            if f == 0:
                body(0)
            with eng.Fori(1 if f == 0 else 0, (NCH - 1) // 2) as i:
                body(i)

        def wait_split(eng, u0, i=0):
            if u0 in POOL_UNITS:
                eng.wait_ge(pool_split, splits(u0))
            else:
                eng.wait_ge(split_ready, splits(u0) + 4 * i)

        def block_columns(ap, b, odd):
            return ap.rearrange("p (n h b) -> p n h b", h=2, b=b)[:, :, odd, :]

        def looped(i):
            return not isinstance(i, int)

        block = ctx.enter_context(nc.Block())

        def raw_wait(u0, i):
            return 32 * (u0 // RING + 1) + 32 * i

        @block.sync
        def _(sp):
            def load(u0, i, src):
                if u0 >= RING or looped(i):
                    wait_split(sp, u0 - RING, i)
                for half in range(2):
                    dst, s = src(half)
                    sp.dma_start(dst(w_raw[u0 % RING]), s).then_inc(raw_loaded[u0 % RING], 16)

            def gate_up(u0, i, w, kh, c):
                v = w.rearrange("(h t p) (g c n) -> h g c p t n", h=2, t=4, p=P, g=2, c=NCH)
                load(u0, i, lambda g: (
                    lambda raw: raw[:].rearrange("p (t g n) -> p t g n", t=4, g=2)[:, :, g, :], v[kh, g, c]))
                if u0 == 0:
                    load_x(1)

            def rows(u0, w, d):
                v = w.rearrange("(d t p) n -> d t p n", t=2, p=P)
                load(u0, 0, lambda t: (lambda raw: raw[:, t * D:(t + 1) * D], v[d, t]))

            def columns(u0, w, kh, col):
                v = w.rearrange("(h s t p) n -> h s p t n", h=2, s=2, t=2, p=P)
                load(u0, 0, lambda s: (
                    lambda raw: raw[:, s * D:(s + 1) * D].rearrange("p (t n) -> p t n", t=2),
                    v[kh, s][:, :, col:col + BANK]))

            def ffn(f, w_gu, w_down):
                u = U_FFN[f]
                for kh in range(2):
                    gate_up(u + kh, 0, w_gu, kh, 0)

                def two_chunks(i):
                    for c in range(2):
                        for kh in range(2):
                            gate_up(u + 2 + 2 * c + kh, i, w_gu, kh, 2 * i + 1 + c)

                rounds(sp, f, two_chunks)
                for d in range(DOWN_UNITS):
                    rows(u + GU_UNITS + d, w_down, d)

            def load_x(t):
                sp.dma_start(x_sb[:, t, :], x[0, t * P:(t + 1) * P, :]).then_inc(x_loaded[t], 16)

            load_x(0)
            for n, w in enumerate([ffn1_norm, mix_norm, ffn2_norm]):
                sp.dma_start(norm_rows[n * 2 * KT:(n + 1) * 2 * KT, :],
                             w.rearrange("l (t p) -> (l t) p", p=P)).then_inc(rows_loaded, 16)
            ffn(0, ffn1_w_gate_up[0], ffn1_w_down[0])
            for n, col in enumerate(ATT_COLS):
                for kh in range(2):
                    columns(U_ATT + 2 * n + kh, attn_w_in[0], kh, col)
            for d in range(OUT_UNITS):
                rows(U_ATT_OUT + d, attn_w_out[0], d)
            ffn(1, ffn2_w_gate_up[0], ffn2_w_down[0])
            ffn(2, ffn1_w_gate_up[1], ffn1_w_down[1])
            for n, col in enumerate(GDN_COLS):
                for kh in range(2):
                    columns(U_GDN + 2 * n + kh, gdn_w_in[0], kh, col)
            for d in range(OUT_UNITS):
                rows(U_GDN_OUT + d, gdn_w_out[0], d)
            ffn(3, ffn2_w_gate_up[1], ffn2_w_down[1])
            for t in range(TT):
                for half in range(2):
                    at = slice(half * BANK, (half + 1) * BANK)
                    sp.wait_ge(y_ready, 2 * t + half + 1)
                    sp.dma_start(out[0, t * P:(t + 1) * P, at], y_sb[:, t, at]).then_inc(out_stored, 16)
            sp.wait_ge(out_stored, 16 * 2 * TT)

        @block.gpsimd
        def _(pool):
            steps = [0]

            def after(ins):
                steps[0] += 1
                ins.then_inc(pool_step, 1)
                pool.wait_ge(pool_step, steps[0])

            after(pool.memset(ident[:], 0.0))
            pool.affine_select(ident[:], ident[:], pattern=[[-1, P]], compare_op=ALU.not_equal, fill=1.0,
                               base=0, channel_multiplier=1).then_inc(ident_ready, 1)

            pool.wait_ge(unit_done, U_ATT)
            for t in range(TT):
                pool.memset(k_pad[t][:], 0.0)
                z = pool.memset(v_pad[t][:], 0.0)
            z.then_inc(a_zero, 1)
            pool.tensor_copy(ident_bf[:], ident[:])
            after(pool.memset(score_mask[:], 0.0))
            pool.affine_select(score_mask[:, 0, :], score_mask[:, 0, :], pattern=[[1, P]],
                               compare_op=ALU.is_gt, fill=MASKED, base=0, channel_multiplier=-1)
            pool.affine_select(score_mask[:, 1, :], score_mask[:, 1, :], pattern=[[-1, P]],
                               compare_op=ALU.is_ge, fill=MASKED, base=0,
                               channel_multiplier=1).then_inc(a_mask, 1)

            def rotate(v, t, heads):
                r1, r2 = v[:, :, 0:ROT], v[:, :, ROT:2 * ROT]
                sin, cos = sincos[:, 0, t, 0:heads, :], sincos[:, 1, t, 0:heads, :]
                m = [r[:, 0:heads, :] for r in rot]
                pool.tensor_tensor(m[0], r1, cos, ALU.mult)
                pool.tensor_tensor(m[1], r2, sin, ALU.mult)
                pool.tensor_tensor(m[2], r2, cos, ALU.mult)
                after(pool.tensor_tensor(m[3], r1, sin, ALU.mult))
                pool.tensor_tensor(r1, m[0], m[1], ALU.subtract)
                return pool.tensor_tensor(r2, m[2], m[3], ALU.add)

            pool.wait_ge(rope_ready, 1)
            for t in range(TT):
                pool.wait_ge(k_row, t + 1)
                after(rotate(k_pad[t][:, :, 0, 0:DH], t, HKV))
                pool.tensor_copy(k_pad[t][:, :, 1, DH:P], k_pad[t][:, :, 0, 0:DH]).then_inc(k_rot, 1)
                pool.wait_ge(v_row, t + 1)
                pool.tensor_copy(v_pad[t][:, :, 1, DH:P], v_pad[t][:, :, 0, 0:DH]).then_inc(v_both, 1)
            for c in range(2):
                for t in range(TT):
                    pool.wait_ge(q_biased, 2 * c + t + 1)
                    rotate(y_sb[:, t, c * BANK:(c + 1) * BANK].rearrange("p (h d) -> p h d", d=DH), t,
                           BANK // DH).then_inc(q_rot, 1)
                    pool.wait_ge(q_rot, 2 * c + t + 1)
            pool.wait_ge(a_loaded, 16 * A_LOADS)
            for t in range(TT):
                pool.wait_ge(xT_psum, 4 * E_ATT + 4)
                pool.wait_ge(ssq_ready, TT * (E_ATT + 1))
                pool.tensor_tensor(x_sb[:, t, :], x_sb[:, t, :], b_out[:], ALU.add).then_inc(bias_added, 1)

            pool.wait_ge(unit_done, U_GDN)
            pool.memset(wba_hi[:].bitcast(F32), 0.0)
            pool.memset(wba_lo[:].bitcast(F32), 0.0).then_inc(wba_zero, 1)
            pool.memset(ones[:], 1.0)
            pool.memset(lower[:], 1.0)
            after(pool.memset(upper[:], 1.0))
            pool.affine_select(lower[:], lower[:], pattern=[[-1, P]], compare_op=ALU.is_ge, fill=0.0,
                               base=0, channel_multiplier=1)
            pool.affine_select(upper[:], upper[:], pattern=[[1, P]], compare_op=ALU.is_ge, fill=0.0,
                               base=0, channel_multiplier=-1)
            after(pool.memset(level1[:], 0.0))
            for b in LEVELS:
                pool.memset(level[b][:], 1.0)
            after(pool.memset(block_columns(level1[:], 1, 0), 1.0))

            views = [(1, block_columns(level1[:], 1, 0)[:, :, 0], lambda sign: [[2 * sign, P // 2]])]
            for b in LEVELS:
                views.append((b, level[b][:].rearrange("p (g n b) -> p g n b", g=HG, b=b),
                              lambda sign, b=b: [[0, HG], [2 * b * sign, P // (2 * b)], [0, b]]))
            for b, v, pattern in views:
                z = pool.affine_select(v, v, pattern=pattern(-1), compare_op=ALU.is_ge,
                                       fill=0.0, base=-b, channel_multiplier=1)
            after(z)
            for b, v, pattern in views:
                z = pool.affine_select(v, v, pattern=pattern(1), compare_op=ALU.is_ge,
                                       fill=0.0, base=2 * b - 1, channel_multiplier=-1)
            z.then_inc(g_masks, 1)

            def split_lo(u):
                pool.wait_ge(hi_ready, u + 1)
                pool.tensor_tensor(w_lo[u % RING][:], w_raw[u % RING][:], w_hi[u % RING][:].bitcast(F32),
                                   ALU.subtract).then_inc(pool_split, 1)

            def decay_rows(g):
                for t in range(TT):
                    for h in range(HG):
                        z = pool.tensor_scalar(gU[:, t, h, :], upper[:], gates[:, 1, t, HG * g + h:HG * g + h + 1],
                                               None, ALU.mult)
                    z.then_inc(gU_ready, 1)

            for g in range(NG):
                if g:
                    pool.wait_ge(R_psum, TT * g)
                    decay_rows(g)
                split_lo(U_GDN + 8 * g + 5)
                if g == 0:
                    pool.wait_ge(gate_dve, GATE_G)
                    decay_rows(g)
                split_lo(U_GDN + 8 * g + 7)
                for t in range(TT):
                    pool.wait_ge(decay_exp, TT * g + t + 1)
                    pool.tensor_tensor(Lm[t][:], Lm[t][:], lower[:].unsqueeze(1).broadcast_to([P, HG, P]),
                                       ALU.mult).then_inc(L_ready, 1)
                split_lo(U_GDN + 8 * g + 9)
                pool.wait_ge(g_loaded, 16 * G_LOADS)
                for t in range(TT):
                    pool.wait_ge(z_silu, TT * g + t + 1)
                    pool.tensor_tensor(y_sb[:, t, 0:HG * DK].rearrange("p (h n) -> p h n", h=HG), y_sb[:, t, 0:HG * DK].rearrange("p (h n) -> p h n", h=HG),
                                       norm_w[:].unsqueeze(1).broadcast_to([P, HG, DK]),
                                       ALU.mult).then_inc(z_ready, 1)
                split_lo(U_GDN + 8 * g + 11)


        @block.scalar
        def _(act):
            def split_hi(u0, i=0):
                act.wait_ge(raw_loaded[u0 % RING], raw_wait(u0, i))
                if u0 >= RING:
                    act.wait_ge(unit_done, u0 - RING + 1 + 4 * i)
                act.activation(w_hi[u0 % RING][:], w_raw[u0 % RING][:], ACT.Copy).then_inc(hi_ready, 1)

            def square(e, t, src, junk):
                act.activation(junk, src, ACT.Square, accum_out=ssq[:, t:t + 1]).then_inc(ssq_ready, 1)

            def root(n, cols=slice(0, TT)):
                act.wait_ge(inv_ready, n)
                act.activation(rstd[:, cols], inv_ms[:, cols], ACT.Sqrt).then_inc(rstd_ready, 1)

            def enter_hi(e, ns=range(4)):
                for n in ns:
                    t, half = quarters(e)[n]
                    act.wait_ge(xT_psum, 4 * e + n + 1)
                    for j in range(4):
                        kt = 4 * half + j
                        z = act.activation(xT_hi[:, kt, t * P:(t + 1) * P],
                                           bank[ENTER_BANKS[t] + half][:, j * P:(j + 1) * P], ACT.Copy,
                                           scale=norm_cols[:, norm_col(e, kt):norm_col(e, kt) + 1])
                    z.then_inc(xT_hi_ready, 1)

            def hT_hi_part(f, j, i):
                act.wait_ge(hT_psum, NCH * f + j + 1 + 2 * i)
                act.activation(hT_hi[:, bass.ds((j + 2 * i) * BANK, BANK)], bank[4 + j % 2][:],
                               ACT.Copy).then_inc(hT_hi_ready, 1)

            def gate_chunk(f, j, i, before):
                u, c = U_FFN[f] + 2 * j, NCH * f + j
                act.wait_ge(unit_done, u + 2 + 4 * i)
                for t in range(TT):
                    if c >= 2 or looped(i):
                        act.wait_ge(h_ready, 2 * (c - 2) + t + 1 + 4 * i)
                    act.activation(silu_g[j % 2][:, t, :], bank[gu_banks(j)[t]][:, 0:FC], ACT.Silu,
                                   scale=rstd[:, t:t + 1]).then_inc(silu_ready, 1)
                split_hi(u + 4, i)
                if before:
                    hT_hi_part(f, j - 1, i)
                split_hi(u + 5, i)

            def ffn(f):
                e, u = E_FFN[f], U_FFN[f]
                if f == 0:
                    enter_hi(e, range(1, 2))
                    split_hi(1)
                    enter_hi(e, range(2, 4))
                    split_hi(2)
                else:
                    enter_hi(e)
                for t in range(TT):
                    square(e, t, x_sb[:, t, :], y_sb[:, t, :])
                split_hi(u + RING - 1)
                if f == 3:
                    act.wait_ge(unit_done, U_FFN[3])
                    act.dma_start(final_w[:], final_norm.rearrange("(o n) -> o n", o=1).broadcast_to([P, D])
                                  ).then_inc(final_loaded, 16)
                root(RSTD_FFN[f])
                act.wait_ge(rstd_ready, RSTD_FFN[f])
                gate_chunk(f, 0, 0, False)
                if f == 0:
                    act.wait_ge(cols_psum, 2)
                    act.activation(conv_cols[:], bank[5][:, 0:CONV_ROWS], ACT.Copy).then_inc(conv_cols_ready, 1)

                def two_chunks(i):
                    gate_chunk(f, 1, i, True)
                    gate_chunk(f, 2, i, True)

                rounds(act, f, two_chunks)
                for d in range(DOWN_UNITS - 1):
                    if u + GU_UNITS + d + RING < U_END:
                        split_hi(u + GU_UNITS + d + RING)
                    if d == 0:
                        hT_hi_part(f, NCH - 1, 0)

            act.dma_start(conv_rows[:],
                          gdn_conv_w[0].rearrange("j (t p) -> (j t) p", p=P)).then_inc(conv_loaded, 16)
            act.wait_ge(cols_psum, 1)
            act.activation(norm_cols[:], bank[0][:, 0:NORM_ROWS], ACT.Copy).then_inc(cols_ready, 1)
            act.wait_ge(cols_ready, 1)
            act.wait_ge(raw_loaded[0], raw_wait(0, 0))
            for j in range(4):
                at = slice(j * BANK, (j + 1) * BANK)
                act.activation(w_hi[0][:, at], w_raw[0][:, at], ACT.Copy).then_inc(first_hi if j < 3 else hi_ready, 1)
                if j == 0:
                    enter_hi(0, range(1))
            ffn(0)

            enter_hi(E_ATT)
            act.wait_ge(unit_done, U_ATT)
            act.dma_start(b_in[:], attn_b_in[0:1, :].broadcast_to([P, 3 * BANK])).then_inc(a_loaded, 16)
            act.dma_start(b_out[:], attn_b_out[0:1, :].broadcast_to([P, D])).then_inc(a_loaded, 16)
            act.dma_start(sink[:], attn_sinks[0:1, :].broadcast_to([P, HQ])).then_inc(a_loaded, 16)
            act.dma_start(pos_i[:], positions.rearrange("o (t p) -> p (o t)", p=P),
                          allow_slow_non_contiguous=True).then_inc(a_loaded, 16)
            for t in range(TT):
                square(E_ATT, t, x_sb[:, t, :], y_sb[:, t, :])
            split_hi(U_ATT + RING - 1)
            root(RSTD_ATT)
            act.wait_ge(angle_ready, 1)
            act.activation(sincos[:].rearrange("p s t h r -> p (s t h r)"),
                           ang[:].rearrange("p s t a -> p (s t a)"), ACT.Sin).then_inc(rope_ready, 1)

            def att_evac(f, dst, src):
                act.wait_ge(a_fill, f + 1)
                act.activation(dst, src, ACT.Copy).then_inc(a_evac, 1)

            split_hi(U_ATT + 4)
            split_hi(U_ATT + 5)
            for f in range(4):
                t, half = f // 2, f % 2
                att_evac(f, kzT[:, 2 * half:2 * half + 2, :, t * P:(t + 1) * P],
                         bank[4 + f % 2][:].rearrange("p (k e n) -> p k e n", k=2, e=2))
            split_hi(U_ATT + 6)

            def q_evac(c, f0):
                for t in range(TT):
                    att_evac(f0 + t, qT[:, 4 * c:4 * c + 4, t * P:(t + 1) * P],
                             bank[4 + (f0 + t) % 2][:].rearrange("p (k n) -> p k n", k=4))

            q_evac(0, 4)
            for s in range(STEPS + 1):
                if s < len(ITEMS):
                    t, p = ITEMS[s]
                    keys = (t + 1) * P
                    pr = prob[s % PROBS]
                    act.wait_ge(max_ready, s + 1)
                    if s >= PROBS:
                        act.wait_ge(a_fill, FILL_NO[ITEM_FILL[s - PROBS]] + 1)
                    for h in range(2):
                        act.activation(pr[:, h, 0:keys], bank[6 + s % 2][:, h * keys:(h + 1) * keys], ACT.Exp,
                                       scale=DH ** -0.5, bias=sm_nmax[:, s, h:h + 1], accum_out=sm_sum[:, s, h:h + 1])
                    act.activation(sm_sink[:, s, :], sm_off[:, s, :], ACT.Exp).then_inc(exp_done, 1)
                for n, items in enumerate(FILLS):
                    if items[-1] == s - 2:
                        if n >= 2:
                            act.wait_ge(pv_done, n - 1)
                        att_evac(FILL_NO[n], probT[n % 2][:], bank[4 + FILL_NO[n] % 2][:])
                if s == Q_STEP:
                    q_evac(1, Q_FILL)
                if s == Q_STEP + 1:
                    split_hi(U_ATT + 7)
                for n, (c, t) in enumerate(OUTS):
                    if s == OUT_STEP[n]:
                        act.wait_ge(pv_done, OUT_PV[n])
                        act.activation(a_oT_hi[:, 4 * c:4 * c + 4, t * P:(t + 1) * P],
                                       bank[2 * c + t][:].rearrange("p (k n) -> p k n", k=4),
                                       ACT.Copy).then_inc(o_hi_ready, 1)
            for n in range(8, 10):
                split_hi(U_ATT + n)
            for d in range(OUT_UNITS - 1):
                split_hi(U_ATT_OUT + d + RING)
            ffn(1)
            ffn(2)

            act.activation(spare[:], norm_cols[:, 0:1], ACT.Sqrt)
            for t in range(TT):
                act.wait_ge(resid_ready, 4 * (E_GDN - 1) + 2 * t + 2)
                square(E_GDN, t, x_sb[:, t, :], y_sb[:, t, :])
                root(RSTD_GDN + t + 1, slice(t, t + 1))
            enter_hi(E_GDN)
            act.wait_ge(unit_done, U_GDN)
            act.dma_start(wba[:], gdn_w_in[0].rearrange("(t p) n -> p t n", p=P)[:, :, 4 * D:4 * D + 2 * GH]
                          ).then_inc(g_loaded, 16)
            act.dma_start(head_vec[:, 0, :], gdn_A_log[0:1, :].broadcast_to([P, GH])).then_inc(g_loaded, 16)
            act.dma_start(head_vec[:, 1, :], gdn_dt_bias[0:1, :].broadcast_to([P, GH])).then_inc(g_loaded, 16)
            act.dma_start(norm_w[:], gdn_norm_w[0:1, :].broadcast_to([P, DK])).then_inc(g_loaded, 16)
            split_hi(U_GDN + RING - 1)
            act.wait_ge(wba_zero, 1)
            act.wait_ge(g_loaded, 16 * G_LOADS)
            act.activation(wba_hi[:, :, 0:2 * GH], wba[:], ACT.Copy).then_inc(wba_hi_ready, 1)

            def conv(g, part, meanwhile=None):
                n = 4 * g + part
                act.wait_ge(unit_done, U_GDN + 2 * n + 2)
                for b in range(2):
                    for h in (2 * b, 2 * b + 1):
                        col = (CONV - 1) * 24 + part * 8 + HG * g + h
                        z = act.activation(cT[part][:, h, :], bank[CONV_BANKS[part][b]][:, (h % 2) * SEQ:(h % 2 + 1) * SEQ],
                                           ACT.Copy, scale=conv_cols[:, col:col + 1])
                    z.then_inc(conv_first, 1)
                split_hi(U_GDN + 2 * n + 4)
                if part < 2:
                    split_hi(U_GDN + 2 * n + 5)
                if meanwhile:
                    meanwhile()
                act.wait_ge(conv_sum, HG * (3 * g + part + 1))
                act.activation(cT[part][:], cT[part][:], ACT.Silu).then_inc(conv_ready, 1)

            def squares(g, f, row, signal):
                t = f % 2
                act.wait_ge(g_fill, FILLS_G * g + f + 1)
                for h in range(HG):
                    z = act.activation(Lm[t][:, h, :], bank[4 + f % 2][:, h * DK:(h + 1) * DK], ACT.Square,
                                       accum_out=sc[:, row, t, h:h + 1])
                z.then_inc(signal, 1)

            def g_copy(g, f, dst):
                act.wait_ge(g_fill, FILLS_G * g + f + 1)
                act.activation(dst, bank[4 + f % 2][:].rearrange("p (h n) -> p h n", h=HG),
                               ACT.Copy).then_inc(g_evac_act, 1)

            def copy(ready, value, dst, b, signal):
                act.wait_ge(ready, value)
                act.activation(dst, bank[b][:].rearrange("p (h n) -> p h n", h=HG), ACT.Copy).then_inc(signal, 1)

            for g in range(NG):
                def b_and_a():
                    act.wait_ge(ba_psum, 1)
                    act.activation(ba_T[:], bank[6][:, 0:SEQ], ACT.Copy).then_inc(ba_ready, 1)

                def k_squares():
                    for t in range(TT):
                        squares(g, FILL_K + t, 1, kq_ssq)

                conv(g, 0, b_and_a if g == 0 else None)
                if g == 0:
                    act.wait_ge(gate_dve, 3)
                    act.activation(gates[:, 7], gates[:, 0], ACT.Exp, scale=-1.0).then_inc(gate_act, 1)
                    act.activation(gates[:, 8], gates[:, 6], ACT.Exp).then_inc(gate_act, 1)
                    act.activation(head_vec[:, 2, :], head_vec[:, 0, :], ACT.Exp).then_inc(gate_act, 1)
                    act.wait_ge(gate_act, 3)
                    act.activation(gates[:, 9], gates[:, 8], ACT.Ln, bias=1.0).then_inc(gate_act, 1)
                    act.wait_ge(gate_dve, 9)
                    act.activation(gates[:, 3], gates[:, 2], ACT.Exp).then_inc(gate_act, 1)
                    act.activation(gates[:, 4], gates[:, 5], ACT.Exp).then_inc(gate_act, 1)
                conv(g, 1)
                for t in range(TT):
                    squares(g, t, 0, g_evac_act)
                conv(g, 2, k_squares)
                act.wait_ge(kq_inv, g + 1)
                act.activation(sc[:, RHO:RK + 1], sc[:, 2:4], ACT.Sqrt).then_inc(kq_root, 1)
                for t in range(TT):
                    act.wait_ge(decay_diff, TT * g + t + 1)
                    act.activation(Lm[t][:], Lm[t][:], ACT.Exp, scale=-1.0).then_inc(decay_exp, 1)
                split_hi(U_GDN + 8 * g + 9)
                act.wait_ge(unit_done, U_GDN + 8 * (g + 1))
                for t in range(TT):
                    if g:
                        act.wait_ge(O_final, TT * g)
                    act.activation(y_sb[:, t, 0:HG * DK].rearrange("p (h n) -> p h n", h=HG), bank[t][:].rearrange("p (h n) -> p h n", h=HG),
                                   ACT.Silu).then_inc(z_silu, 1)
                split_hi(U_GDN + 8 * g + 10)
                for t in range(TT):
                    g_copy(g, FILL_A + t, AT[t][:])
                for t in range(TT):
                    g_copy(g, FILL_X + t, XT[t][:])
                for t in range(TT):
                    g_copy(g, FILL_AQK + t, AqkT[t][:])
                for t in range(TT):
                    act.wait_ge(g_fill, FILLS_G * g + FILL_V + t + 1)
                    for h in range(HG):
                        z = act.activation(v_beta[:, t, h, :], bank[4 + t][:, h * DK:(h + 1) * DK], ACT.Copy,
                                           scale=sc[:, 4, t, h:h + 1])
                    z.then_inc(g_evac_act, 1)
                for n in range(1, len(LEVELS)):
                    for t in range(TT):
                        copy(XT_psum, TT * ((len(LEVELS) - 1) * g + n - 1) + t + 1, XT[t][:], ZT_BANK[t], XT_copied)
                split_hi(U_GDN + 8 * g + 11)
                copy(U_psum, TT * g + 1, Y[0][:], U_BANK[0], U_ready)
                copy(W_psum, g + 1, X[1][:], W_BANK, W_ready)
                copy(S_psum, g + 1, X[0][:], S_BANK, S_ready)
                copy(U_psum, TT * g + 2, Y[1][:], U_BANK[1], U_ready)
                for t in range(TT):
                    act.wait_ge(O_ready, TT * g + t + 1)
                    for h in range(HG):
                        z = act.activation(AT[t][:, h, :], Lm[t][:, h, :], ACT.Square, accum_out=sc[:, 8, t, h:h + 1])
                    z.then_inc(O_ssq, 1)
                act.wait_ge(o_inv, g + 1)
                act.activation(sc[:, 7], sc[:, 11], ACT.Sqrt).then_inc(o_root, 1)
                for t in range(TT):
                    act.wait_ge(g_fill, FILLS_G * g + FILL_O + t + 1)
                    act.activation(g_oT_hi[:, HG * g:HG * (g + 1), t * P:(t + 1) * P],
                                   bank[4 + t][:].rearrange("p (h n) -> p h n", h=HG),
                                   ACT.Copy).then_inc(o_hi_ready, 1)
            for d in range(OUT_UNITS - 1):
                split_hi(U_GDN_OUT + d + RING)
            ffn(3)
            act.activation(spare[:], norm_cols[:, 0:1], ACT.Sqrt)
            for t in range(TT):
                act.wait_ge(resid_ready, 4 * 5 + 2 * t + 2)
                square(6, t, x_sb[:, t, :], y_sb[:, t, :])
                root(RSTD_FINAL + t + 1, slice(t, t + 1))

        @block.vector
        def _(dve):
            steps = [0]

            def after(ins):
                steps[0] += 1
                ins.then_inc(vec_step, 1)
                dve.wait_ge(vec_step, steps[0])

            def split_lo(u0, i=0):
                dve.wait_ge(hi_ready, u0 + 1 + 4 * i)
                dve.tensor_tensor(w_lo[u0 % RING][:], w_raw[u0 % RING][:], w_hi[u0 % RING][:].bitcast(F32),
                                  ALU.subtract).then_inc(split_ready, 1)

            def residual(e, n, factor):
                t, half = quarters(e)[n]
                if n < 3:
                    dve.wait_ge(acc_done, 3 * (e - 1) + n + 1)
                else:
                    dve.wait_ge(unit_done, RESIDUAL_UNIT[e - 1])
                dve.scalar_tensor_tensor(x_sb[:, t, half * BANK:(half + 1) * BANK], bank[ACC[t][half]][:],
                                         factor, x_sb[:, t, half * BANK:(half + 1) * BANK],
                                         ALU.mult, ALU.add).then_inc(resid_ready, 1)

            def enter_lo(e, n):
                t, half = quarters(e)[n]
                dve.wait_ge(xT_hi_ready, 4 * e + n + 1)
                for j in range(4):
                    kt = 4 * half + j
                    z = dve.scalar_tensor_tensor(
                        xT_lo[:, kt, t * P:(t + 1) * P], bank[ENTER_BANKS[t] + half][:, j * P:(j + 1) * P],
                        norm_cols[:, norm_col(e, kt):norm_col(e, kt) + 1],
                        xT_hi[:, kt, t * P:(t + 1) * P].bitcast(F32), ALU.mult, ALU.subtract)
                z.then_inc(xT_lo_ready, 1)

            def inverse_rms(count, cols=slice(0, TT)):
                dve.wait_ge(ssq_ready, count)
                after(dve.tensor_scalar(mean_sq[:, cols], ssq[:, cols], 1.0 / D, EPS, ALU.mult, ALU.add))
                dve.reciprocal(inv_ms[:, cols], mean_sq[:, cols]).then_inc(inv_ready, 1)

            def hT_lo_part(f, j, i):
                dve.wait_ge(hT_hi_ready, NCH * f + j + 1 + 2 * i)
                at = bass.ds((j + 2 * i) * BANK, BANK)
                dve.tensor_tensor(hT_lo[:, at], bank[4 + j % 2][:], hT_hi[:, at].bitcast(F32),
                                  ALU.subtract).then_inc(hT_lo_ready, 1)

            def gate_chunk(f, j, i, before):
                u, c = U_FFN[f] + 2 * j, NCH * f + j
                for t in range(TT):
                    dve.wait_ge(silu_ready, 2 * c + t + 1 + 4 * i)
                    if t == 0 and (c >= 2 or looped(i)):
                        dve.wait_ge(hT_psum, c - 1 + 2 * i)
                    dve.scalar_tensor_tensor(h_row[j % 2][:, t, :], bank[gu_banks(j)[t]][:, FC:2 * FC],
                                             rstd[:, t:t + 1], silu_g[j % 2][:, t, :],
                                             ALU.mult, ALU.mult).then_inc(h_ready, 1)
                split_lo(u + 4, i)
                if before:
                    hT_lo_part(f, j - 1, i)
                split_lo(u + 5, i)

            def enter(e, factor, scaled=False):
                if scaled:
                    for t in range(TT):
                        for half in range(2):
                            residual(e, 2 * t + half, factor)
                        inverse_rms(TT * e + t + 1, slice(t, t + 1))
                        dve.wait_ge(rstd_ready, RSTD_GDN + t + 1)
                        dve.tensor_scalar(diag_rstd[:, t, :], ident[:], rstd[:, t:t + 1], None,
                                          ALU.mult).then_inc(diag_ready, 1)
                    for n in range(4):
                        enter_lo(e, n)
                    split_lo(PHASE_UNIT[e] + 2)
                else:
                    if e:
                        for n in range(3):
                            residual(e, n, factor)
                        enter_lo(e, 0)
                    enter_lo(e, 1)
                    if e:
                        residual(e, 3, factor)
                    else:
                        split_lo(1)
                    enter_lo(e, 2)
                    enter_lo(e, 3)
                    split_lo(PHASE_UNIT[e] + 2)
                    inverse_rms(TT * (e + 1))

            def ffn(f, factor):
                u = U_FFN[f]
                enter(E_FFN[f], factor)
                split_lo(u + RING - 1)
                dve.wait_ge(rstd_ready, RSTD_FFN[f])
                gate_chunk(f, 0, 0, False)

                def two_chunks(i):
                    gate_chunk(f, 1, i, True)
                    gate_chunk(f, 2, i, True)

                rounds(dve, f, two_chunks)
                for d in range(DOWN_UNITS - 2):
                    if u + GU_UNITS + d + RING < U_END:
                        split_lo(u + GU_UNITS + d + RING)
                    if d == 0:
                        hT_lo_part(f, NCH - 1, 0)

            dve.wait_ge(cols_ready, 1)
            for j in range(4):
                at = slice(j * BANK, (j + 1) * BANK)
                if j < 3:
                    dve.wait_ge(first_hi, j + 1)
                else:
                    dve.wait_ge(hi_ready, 1)
                dve.tensor_tensor(w_lo[0][:, at], w_raw[0][:, at], w_hi[0][:, at].bitcast(F32),
                                  ALU.subtract).then_inc(first_split if j < 3 else split_ready, 1)
                if j == 0:
                    enter_lo(0, 0)
            ffn(0, None)

            enter(E_ATT, 0.5)
            split_lo(U_ATT + RING - 1)
            dve.wait_ge(a_loaded, 16 * A_LOADS)
            dve.tensor_scalar(nsink[:], sink[:], -1.0, None, ALU.mult)
            for r in range(ROT):
                dve.memset(invf[:, :, r:r + 1], float(INV_FREQ[r]))
            after(dve.tensor_copy(pos_f[:], pos_i[:]))
            for t in range(TT):
                z = dve.tensor_scalar(ang[:, 0, t, :], invf[:].rearrange("p h r -> p (h r)"), pos_f[:, t:t + 1],
                                      None, ALU.mult)
            after(z)
            after(dve.tensor_scalar(ang[:, 1], ang[:, 0], 0.0, None, ALU.add))
            dve.tensor_scalar(turns[:, 0], ang[:, 0], 1.0 / TWO_PI, None, ALU.mult)
            after(dve.tensor_scalar(turns[:, 1], ang[:, 1], 1.0 / TWO_PI, 0.25, ALU.mult, ALU.add))
            after(dve.tensor_scalar(turns[:], turns[:], ROUND, None, ALU.add))
            after(dve.tensor_scalar(turns[:], turns[:], ROUND, None, ALU.subtract))
            for part in TURN:
                after(dve.scalar_tensor_tensor(ang[:], turns[:], -part, ang[:], ALU.mult, ALU.add))
            after(dve.tensor_scalar(ang[:, 1], ang[:, 1], TWO_PI / 4, None, ALU.add))
            dve.tensor_scalar(ang[:], ang[:], PI_BELOW, -PI_BELOW, ALU.min, ALU.max).then_inc(angle_ready, 1)

            dve.wait_ge(unit_done, U_ATT + 2)
            dve.wait_ge(a_zero, 1)
            dve.wait_ge(rstd_ready, RSTD_ATT)
            for t in range(TT):
                for dst, col, signal in ((k_pad, 0, k_row), (v_pad, HKV * DH, v_row)):
                    dve.scalar_tensor_tensor(
                        dst[t][:, :, 0, 0:DH], bank[ATT_BANKS[0][t]][:, col:col + HKV * DH].rearrange(
                            "p (h d) -> p h d", d=DH), rstd[:, t:t + 1],
                        b_in[:, D + col:D + col + HKV * DH].rearrange("p (h d) -> p h d", d=DH),
                        ALU.mult, ALU.add).then_inc(signal, 1)
            split_lo(U_ATT + 4)
            split_lo(U_ATT + 5)
            def q_bias(c):
                dve.wait_ge(unit_done, U_ATT + 4 + 2 * c)
                for t in range(TT):
                    dve.scalar_tensor_tensor(y_sb[:, t, c * BANK:(c + 1) * BANK], bank[ATT_BANKS[1 + c][t]][:], rstd[:, t:t + 1],
                                             b_in[:, c * BANK:(c + 1) * BANK], ALU.mult,
                                             ALU.add).then_inc(q_biased, 1)

            q_bias(0)
            split_lo(U_ATT + 6)
            for s in range(STEPS + 1):
                if s < len(ITEMS):
                    t, p = ITEMS[s]
                    keys = (t + 1) * P
                    dve.wait_ge(score_done, s + 1)
                    after(dve.tensor_reduce(sm_max[:, s, :], bank[6 + s % 2][:, 0:2 * keys].rearrange(
                        "p (h k) -> p h k", h=2), AX, ALU.max))
                    after(dve.scalar_tensor_tensor(sm_nmax[:, s, :], sm_max[:, s, :], -DH ** -0.5,
                                                   nsink[:, 2 * p:2 * p + 2], ALU.mult, ALU.min))
                    dve.tensor_tensor(sm_off[:, s, :], sink[:, 2 * p:2 * p + 2], sm_nmax[:, s, :],
                                      ALU.add).then_inc(max_ready, 1)
                if 0 < s <= len(ITEMS):
                    i = s - 1
                    t, p = ITEMS[i]
                    keys = (t + 1) * P
                    dve.wait_ge(exp_done, i + 1)
                    after(dve.tensor_tensor(sm_total[:, i, :], sm_sum[:, i, :], sm_sink[:, i, :], ALU.add))
                    after(dve.reciprocal(sm_inv[:, i, :], sm_total[:, i, :]))
                    for h in range(2):
                        z = dve.tensor_scalar(prob[i % PROBS][:, h, 0:keys], prob[i % PROBS][:, h, 0:keys],
                                              sm_inv[:, i, h:h + 1], None, ALU.mult)
                    z.then_inc(prob_ready, 1)
                if s == Q_BIAS_STEP:
                    q_bias(1)
                if s == Q_STEP + 2:
                    split_lo(U_ATT + 7)
                for n, (c, t) in enumerate(OUTS):
                    if s == OUT_STEP[n]:
                        dve.wait_ge(o_hi_ready, n + 1)
                        dst = slice(t * P, (t + 1) * P)
                        dve.tensor_tensor(a_oT_lo[:, 4 * c:4 * c + 4, dst],
                                          bank[2 * c + t][:].rearrange("p (k n) -> p k n", k=4),
                                          a_oT_hi[:, 4 * c:4 * c + 4, dst].bitcast(F32),
                                          ALU.subtract).then_inc(o_lo_ready, 1)
            for n in range(8, 10):
                split_lo(U_ATT + n)
            for d in range(OUT_UNITS - 2):
                split_lo(U_ATT_OUT + d + RING)
            dve.wait_ge(bias_added, TT)
            ffn(1, 1.0)
            ffn(2, 0.5)

            dve.wait_ge(conv_cols_ready, 1)
            enter(E_GDN, 0.5, scaled=True)
            split_lo(U_GDN + RING - 1)
            dve.wait_ge(wba_hi_ready, 1)
            dve.tensor_tensor(wba_lo[:, :, 0:2 * GH], wba[:], wba_hi[:, :, 0:2 * GH].bitcast(F32),
                              ALU.subtract).then_inc(wba_ready, 1)

            def conv(g, part):
                n = 4 * g + part
                for shift in range(1, CONV):
                    for h in range(HG):
                        if shift == 1 and h % 2 == 0:
                            dve.wait_ge(conv_first, 2 * (3 * g + part) + h // 2 + 1)
                        col = (CONV - 1 - shift) * 24 + part * 8 + HG * g + h
                        src = bank[CONV_BANKS[part][h // 2]]
                        z = dve.scalar_tensor_tensor(
                            cT[part][:, h, shift:SEQ], src[:, (h % 2) * SEQ:(h % 2 + 1) * SEQ - shift],
                            conv_cols[:, col:col + 1], cT[part][:, h, shift:SEQ], ALU.mult, ALU.add)
                        if shift == CONV - 1:
                            z.then_inc(conv_sum, 1)
                        elif h == HG - 1:
                            after(z)
                if part < 2:
                    split_lo(U_GDN + 2 * n + 4)

            def gate(ins):
                gsteps[0] += 1
                ins.then_inc(gate_dve, 1)
                return gsteps[0]

            def flat(heads):
                return heads[:].rearrange("p h n -> p (h n)")

            def narrow(b, size):
                return bank[b][:, 0:HG * P // 2].rearrange("p (m b) -> p m b", b=size)

            gsteps = [0]
            for g in range(NG):
                hs = slice(HG * g, HG * (g + 1))
                conv(g, 0)
                if g == 0:
                    dve.wait_ge(dec_psum, 1)
                    dve.wait_ge(g_loaded, 16 * G_LOADS)
                    ba = bank[7][:, 0:TT * P].rearrange("p (t c) -> p t c", t=TT)
                    gate(dve.tensor_tensor(gates[:, 5], ba[:, :, GH:2 * GH],
                                           head_vec[:, 1, :].unsqueeze(1).broadcast_to([P, TT, GH]), ALU.add))
                    dve.wait_ge(gate_dve, gate(dve.tensor_copy(gates[:, 0], ba[:, :, 0:GH])))
                    gate(dve.scalar_tensor_tensor(gates[:, 6], gates[:, 5], -1.0, gates[:, 5], ALU.mult, ALU.min))
                    dve.wait_ge(gate_act, 4)
                    dve.wait_ge(gate_dve, gate(dve.tensor_scalar(gates[:, 7], gates[:, 7], 1.0, None, ALU.add)))
                    gate(dve.reciprocal(gates[:, 0], gates[:, 7]))
                    dve.wait_ge(gate_dve, gate(dve.scalar_tensor_tensor(
                        gates[:, 6], gates[:, 5], 0.0, gates[:, 9], ALU.max, ALU.add)))
                    assert gate(dve.scalar_tensor_tensor(
                        gates[:, 1], gates[:, 6], -1.0, head_vec[:, 2, :].unsqueeze(1).broadcast_to([P, TT, GH]),
                        ALU.mult, ALU.mult)) == GATE_G
                    dve.wait_ge(dec_psum, 2)
                    sums = bank[6][:, 0:2 * TT * GH].rearrange("p (s t h) -> p s t h", s=2, t=TT)
                    dve.wait_ge(gate_dve, gate(dve.tensor_copy(gates[:, 2], sums[:, 0])))
                    gate(dve.tensor_tensor(gates[:, 5], sums[:, 1], gates[:, 2], ALU.subtract))
                    dve.wait_ge(gate_act, 6)
                conv(g, 1)
                conv(g, 2)
                dve.wait_ge(g_evac_act, EVACS_G * g + 2)
                dve.wait_ge(kq_ssq, TT * (g + 1))
                dve.tensor_scalar(sc[:, 2], sc[:, 0], float(DK), float(DK) * EPS, ALU.mult, ALU.add)
                after(dve.tensor_scalar(sc[:, 3], sc[:, 1], EPS, None, ALU.add))
                dve.reciprocal(sc[:, 2:4], sc[:, 2:4]).then_inc(kq_inv, 1)
                for t in range(TT):
                    dve.wait_ge(R_psum, TT * g + t + 1)
                    for h in range(HG):
                        z = dve.tensor_scalar(Lm[t][:, h, :], bank[R_BANK[t]][:, h * P:(h + 1) * P],
                                              gates[:, 2, t, HG * g + h:HG * g + h + 1], 0.0,
                                              ALU.subtract, ALU.max)
                    z.then_inc(decay_diff, 1)
                dve.wait_ge(kq_root, g + 1)
                after(dve.tensor_tensor(sc[:, 4], sc[:, RK], gates[:, 0, :, hs], ALU.mult))
                after(dve.tensor_tensor(sc[:, 5], sc[:, 4], sc[:, RK], ALU.mult))
                after(dve.scalar_tensor_tensor(sc[:, 6], sc[:, 5], -1.0, gates[:, 3, :, hs], ALU.mult, ALU.mult))
                for h in range(HG):
                    z = dve.tensor_scalar(k_dec[:, h, :], bank[4][:, h * DK:(h + 1) * DK],
                                          gates[:, 4, 0, HG * g + h:HG * g + h + 1], None, ALU.mult)
                z.then_inc(g_evac_vec, 1)
                for h in range(HG):
                    z = dve.tensor_scalar(k_w[:, h, :], bank[5][:, h * DK:(h + 1) * DK],
                                          sc[:, 6, 1, h:h + 1], None, ALU.mult)
                z.then_inc(g_evac_vec, 1)
                for t in range(TT):
                    dve.wait_ge(L_ready, TT * g + t + 1)
                    dve.wait_ge(KK_psum, TT * g + t + 1)
                    for h in range(HG):
                        z = dve.scalar_tensor_tensor(Y[t][:, h, :], bank[KK_BANK[t]][:, h * P:(h + 1) * P],
                                                     sc[:, 5, t, h:h + 1], Lm[t][:, h, :], ALU.mult, ALU.mult)
                    z.then_inc(A_ready, 1)
                for t in range(TT):
                    dve.wait_ge(A_ready, TT * g + t + 1)
                    after(dve.tensor_tensor(X[t][:], Y[t][:], level1[:].unsqueeze(1).broadcast_to([P, HG, P]),
                                            ALU.mult))
                    dve.scalar_tensor_tensor(X[t][:], X[t][:], -1.0,
                                             ident[:].unsqueeze(1).broadcast_to([P, HG, P]),
                                             ALU.mult, ALU.add).then_inc(X_ready, 1)
                for t in range(TT):
                    dve.wait_ge(QK_psum, TT * g + t + 1)
                    dve.tensor_tensor(Lm[t][:].rearrange("p h n -> p (h n)"), bank[QK_BANK[t]][:],
                                      Lm[t][:].rearrange("p h n -> p (h n)"), ALU.mult).then_inc(Aqk_ready, 1)
                nl = len(LEVELS)
                for n, b in enumerate(LEVELS):
                    for t in range(TT):
                        dve.wait_ge(Y_psum, TT * (nl * g + n) + t + 1)
                        dve.tensor_tensor(block_columns(flat(Y[t]), b, 0), narrow(Y_BANK[t], b),
                                          level[b][:].rearrange("p (m b) -> p m b", b=b),
                                          ALU.mult).then_inc(Y_ready, 1)
                    for t in range(TT):
                        if n < nl - 1:
                            dve.wait_ge(Z_psum, TT * ((nl - 1) * g + n) + t + 1)
                            dve.tensor_tensor(block_columns(flat(X[t]), b, 0), block_columns(flat(X[t]), b, 0),
                                              narrow(Z_BANK[t], b), ALU.subtract).then_inc(X_ready, 1)
                        else:
                            dve.wait_ge(ZT_psum, TT * g + t + 1)
                            dve.tensor_tensor(
                                block_columns(flat(XT[t]), b, 1)[0:b], block_columns(flat(XT[t]), b, 1)[0:b],
                                narrow(ZT_BANK[t], b)[0:b], ALU.subtract).then_inc(XT_ready, 1)
                split_lo(U_GDN + 8 * g + 8)
                dve.wait_ge(O_psum, TT * g + 1)
                dve.tensor_copy(Lm[0][:].rearrange("p h n -> p (h n)"), bank[O_BANK[0]][:]).then_inc(O_ready, 1)
                dve.wait_ge(QS_psum, g + 1)
                for h in range(HG):
                    z = dve.tensor_scalar(Lm[1][:, h, :], bank[QS_BANK][:, h * P:(h + 1) * P],
                                          gates[:, 3, 1, HG * g + h:HG * g + h + 1], None, ALU.mult)
                z.then_inc(QS_ready, 1)
                dve.wait_ge(QS_ready, g + 1)
                dve.wait_ge(O_psum, TT * g + 2)
                dve.tensor_tensor(Lm[1][:].rearrange("p h n -> p (h n)"),
                                  Lm[1][:].rearrange("p h n -> p (h n)"), bank[O_BANK[1]][:],
                                  ALU.add).then_inc(O_ready, 1)
                after(dve.tensor_tensor(sc[:, 9], sc[:, RHO], sc[:, RHO], ALU.mult))
                dve.wait_ge(O_ssq, TT * (g + 1))
                after(dve.scalar_tensor_tensor(sc[:, 10], sc[:, 8], 1.0 / DK, sc[:, 9], ALU.mult, ALU.mult))
                after(dve.tensor_scalar(sc[:, 10], sc[:, 10], EPS, None, ALU.add))
                dve.reciprocal(sc[:, 11], sc[:, 10]).then_inc(o_inv, 1)
                dve.wait_ge(o_root, g + 1)
                after(dve.tensor_tensor(sc[:, 10], sc[:, 7], sc[:, RHO], ALU.mult))
                for t in range(TT):
                    dve.wait_ge(z_ready, TT * g + t + 1)
                    for h in range(HG):
                        z = dve.scalar_tensor_tensor(Lm[t][:, h, :], Lm[t][:, h, :], sc[:, 10, t, h:h + 1],
                                                     y_sb[:, t, h * DK:(h + 1) * DK], ALU.mult, ALU.mult)
                    z.then_inc(O_final, 1)
                split_lo(U_GDN + 8 * g + 10)
                for t in range(TT):
                    dve.wait_ge(o_hi_ready, 4 + TT * g + t + 1)
                    dst = slice(t * P, (t + 1) * P)
                    dve.tensor_tensor(g_oT_lo[:, HG * g:HG * (g + 1), dst],
                                      bank[4 + t][:].rearrange("p (h n) -> p h n", h=HG),
                                      g_oT_hi[:, HG * g:HG * (g + 1), dst].bitcast(F32),
                                      ALU.subtract).then_inc(o_lo_ready, 1)
            for d in range(OUT_UNITS - 2):
                split_lo(U_GDN_OUT + d + RING)
            ffn(3, 1.0)

            dve.wait_ge(final_loaded, 16)
            for t in range(TT):
                for half in range(2):
                    residual(6, 2 * t + half, 0.5)
                inverse_rms(TT * 6 + t + 1, slice(t, t + 1))
                dve.wait_ge(rstd_ready, RSTD_FINAL + t + 1)
                for half in range(2):
                    at = slice(half * BANK, (half + 1) * BANK)
                    dve.scalar_tensor_tensor(y_sb[:, t, at], x_sb[:, t, at], rstd[:, t:t + 1], final_w[:, at],
                                             ALU.mult, ALU.mult).then_inc(y_ready, 1)

        @block.tensor
        def _(pe):
            def products(out_ap, a, b, start, stop, **kw):
                pe.matmul(out_ap, a[0], b[0], start=start, stop=False, **kw)
                pe.matmul(out_ap, a[0], b[1], start=False, stop=False, **kw)
                return pe.matmul(out_ap, a[1], b[0], start=False, stop=stop, **kw)

            def xT(kt, t):
                at = slice(t * P, (t + 1) * P)
                return xT_hi[:, kt, at], xT_lo[:, kt, at]

            def ring(u0, at):
                return w_hi[u0 % RING][:, at], w_lo[u0 % RING][:, at]

            def enter(e, n):
                t, half = quarters(e)[n]
                if e == 0:
                    pe.wait_ge(x_loaded[t], 16)
                elif e == E_GDN:
                    pe.wait_ge(diag_ready, t + 1)
                else:
                    pe.wait_ge(resid_ready, 4 * (e - 1) + n + 1)
                for j in range(4):
                    kt = 4 * half + j
                    dst = bank[ENTER_BANKS[t] + half][:, j * P:(j + 1) * P]
                    src = x_sb[:, t, kt * P:(kt + 1) * P]
                    if e == E_GDN:
                        z = pe.matmul(dst, src, diag_rstd[:, t, :], start=True, stop=True)
                    else:
                        z = pe.transpose(dst, src, ident[:])
                z.then_inc(xT_psum, 1)

            def in_unit(u0, i, kh, banks, e=None):
                if u0 or looped(i):
                    wait_split(pe, u0, i)
                for t in range(TT):
                    if e is not None:
                        pe.wait_ge(xT_lo_ready, 4 * e + quarters(e).index((t, kh)) + 1)
                    for j in range(4):
                        if u0 == 0 and not looped(i) and t == 0:
                            if j < 3:
                                pe.wait_ge(first_split, j + 1)
                            else:
                                wait_split(pe, u0)
                        z = products(bank[banks[t]][:], xT(4 * kh + j, t), ring(u0, slice(j * BANK, (j + 1) * BANK)),
                                     start=(kh == 0 and j == 0), stop=(kh == 1 and j == 3))
                        if e == 0 and kh == 0 and t == 0 and j >= 2:
                            enter(e, j)
                    if t == TT - 1:
                        z.then_inc(unit_done, 1)
                    if e and kh == 0:
                        enter(e, 2 + t)

            def gate_chunk(f, j, i):
                u, c = U_FFN[f] + 2 * j, NCH * f + j
                if j and (c >= 2 or looped(i)):
                    pe.wait_ge(h_ready, 2 * (c - 1) + 4 * i)
                for kh in range(2):
                    in_unit(u + kh, i, kh, gu_banks(j), E_FFN[f] if j == 0 else None)

            def h_transposes(f, j, i):
                c = NCH * f + j
                pe.wait_ge(h_ready, 2 * c + 2 + 4 * i)
                for k in range(2):
                    for t in range(TT):
                        z = pe.transpose(bank[4 + j % 2][:, k * SEQ + t * P:k * SEQ + (t + 1) * P],
                                         h_row[j % 2][:, t, k * P:(k + 1) * P], ident[:])
                z.then_inc(hT_psum, 1)

            def out_unit(u0, d, n, operand, ready, e, tiles=(0, 1)):
                wait_split(pe, u0 + d)
                for m, (t, half) in enumerate(quarters(e)):
                    if t not in tiles:
                        continue
                    ready(2 * d, t)
                    for j in range(2):
                        kt = 2 * d + j
                        z = products(bank[ACC[t][half]][:], operand(kt, t),
                                     ring(u0 + d, slice(j * D + half * BANK, j * D + (half + 1) * BANK)),
                                     start=(kt == 0), stop=(kt == 2 * n - 1))
                        if d == n - 1 and m == 2 and j == 0 and e not in (E_GDN, 6):
                            enter(e, 0)
                    if m == 3 or m == 2 and len(tiles) == 1:
                        z.then_inc(unit_done, 1)
                    elif d == n - 1:
                        z.then_inc(acc_done, 1)
                        if m == 2 and e not in (E_GDN, 6):
                            enter(e, 1)
                if d == n - 1 and e == E_GDN:
                    for m in range(4):
                        enter(e, m)

            def hT(kt, t):
                at = slice(kt * SEQ + t * P, kt * SEQ + (t + 1) * P)
                return hT_hi[:, at], hT_lo[:, at]

            def ffn(f, e_next):
                gate_chunk(f, 0, 0)
                if f == 0:
                    pe.wait_ge(conv_loaded, 16)
                    pe.transpose(bank[5][:, 0:CONV_ROWS], conv_rows[:],
                                 ident[0:CONV_ROWS, 0:CONV_ROWS]).then_inc(cols_psum, 1)

                def two_chunks(i):
                    gate_chunk(f, 1, i)
                    h_transposes(f, 0, i)
                    gate_chunk(f, 2, i)
                    h_transposes(f, 1, i)

                rounds(pe, f, two_chunks)
                for d in range(DOWN_UNITS):
                    out_unit(U_FFN[f] + GU_UNITS, d, DOWN_UNITS, hT,
                             lambda kt, t: pe.wait_ge(hT_lo_ready, NCH * f + kt // 2 + 1), e_next)
                    if d == 1:
                        h_transposes(f, NCH - 1, 0)

            pe.wait_ge(ident_ready, 1)
            pe.wait_ge(rows_loaded, 16 * 3)
            pe.transpose(bank[0][:, 0:NORM_ROWS], norm_rows[:], ident[0:NORM_ROWS, 0:NORM_ROWS]).then_inc(cols_psum, 1)
            for n in range(2):
                enter(0, n)
            ffn(0, E_ATT)

            def a_bank(f):
                if f >= 2:
                    pe.wait_ge(a_evac, f - 1)
                return bank[4 + f % 2]

            def a_fill4(f, sources):
                b = a_bank(f)
                for n, s in enumerate(sources):
                    z = pe.transpose(b[:, n * P:(n + 1) * P], s, ident[:])
                z.then_inc(a_fill, 1)

            def q_part(ms):
                for m in ms:
                    kh, t, j = m // 8, m // 4 % 2, m % 4
                    if m % 8 == 0:
                        wait_split(pe, U_ATT + 4 + kh)
                    z = products(bank[ATT_BANKS[2][t]][:], xT(4 * kh + j, t),
                                 ring(U_ATT + 4 + kh, slice(j * BANK, (j + 1) * BANK)),
                                 start=(kh == 0 and j == 0), stop=(kh == 1 and j == 3))
                    if m % 8 == 7:
                        z.then_inc(unit_done, 1)

            def att_o(kt, t):
                at = slice(t * P, (t + 1) * P)
                return a_oT_hi[:, kt, at], a_oT_lo[:, kt, at]

            def out_part(ms):
                for m in ms:
                    d, half, j = m // 4, m // 2 % 2, m % 2
                    if m == 0:
                        pe.wait_ge(o_lo_ready, 2)
                    if m % 4 == 0:
                        wait_split(pe, U_ATT_OUT + d)
                    products(bank[ACC[1][half]][:], att_o(2 * d + j, 1),
                             ring(U_ATT_OUT + d, slice(j * D + half * BANK, j * D + (half + 1) * BANK)),
                             start=(m % 2 == 0 and d == 0), stop=False)

            def q_fills(c, f):
                for t in range(TT):
                    pe.wait_ge(q_rot, 2 * c + t + 1)
                    a_fill4(f + t, [y_sb[:, t, c * BANK + m * P:c * BANK + (m + 1) * P] for m in range(4)])

            for n in range(2):
                for kh in range(2):
                    in_unit(U_ATT + 2 * n + kh, 0, kh, ATT_BANKS[n], E_ATT if n == 0 else None)
            for t in range(TT):
                pe.wait_ge(k_rot, t + 1)
                for half in range(2):
                    a_fill4(2 * t + half, [k_pad[t][:, 2 * half + m // 2, m % 2, :] for m in range(4)])
                q_part(range(4 * t, 4 * t + 4))
            q_fills(0, 4)
            q_part(range(8, Q_FIRST))
            pe.wait_ge(v_both, TT)
            pe.wait_ge(a_mask, 1)
            for s in range(STEPS):
                if s < len(ITEMS):
                    t, p = ITEMS[s]
                    pe.wait_ge(a_evac, FIRST_FILLS if p < HALF_PAIRS else Q_FILL + 2)
                    if s >= 2:
                        pe.wait_ge(exp_done, s - 1)
                    keys = (t + 1) * P
                    both = bank[6 + s % 2][:, 0:2 * keys].rearrange("p (h k) -> p h k", h=2)
                    mask = score_mask[:, 1 - t:2, :].rearrange("p b k -> p (b k)")
                    pe.matmul(both, ident_bf[:], mask.unsqueeze(1).broadcast_to([P, 2, keys]), start=True, stop=False)
                    pe.matmul(both, qT[:, p, t * P:(t + 1) * P], kzT[:, p // 2, :, 0:keys],
                              start=False, stop=True).then_inc(score_done, 1)
                if s < len(Q_PARTS):
                    m = Q_FIRST + sum(Q_PARTS[:s])
                    q_part(range(m, m + Q_PARTS[s]))
                for n, items in enumerate(FILLS):
                    t, p = ITEMS[items[0]]
                    if items[-1] == s - 2:
                        pe.wait_ge(prob_ready, items[-1] + 1)
                        if t == 0:
                            a_fill4(FILL_NO[n], [prob[i % PROBS][:, h, 0:P] for h in range(2) for i in items])
                        else:
                            a_fill4(FILL_NO[n], [prob[items[0] % PROBS][:, h, b * P:(b + 1) * P]
                                            for h in range(2) for b in range(2)])
                if s == Q_STEP:
                    q_fills(1, Q_FILL)
                for n, items in enumerate(FILLS):
                    t, p = ITEMS[items[0]]
                    if items[-1] == s - 3:
                        pe.wait_ge(a_evac, FILL_NO[n] + 1)
                        pT = probT[n % 2]
                        b_out_T = bank[2 * (p // HALF_PAIRS) + t]
                        if t == 0:
                            kv = p // 2
                            o = b_out_T[:, (p % 4) * P:(p % 4 + 2) * P]
                            pe.matmul(o, v_pad[0][:, kv, 0, :], pT[:, 0:2 * P], start=True, stop=False)
                            z = pe.matmul(o, v_pad[0][:, kv, 1, :], pT[:, 2 * P:4 * P], start=False, stop=True)
                        else:
                            o = b_out_T[:, (p % 4) * P:(p % 4 + 1) * P]
                            for m in range(4):
                                h, b = m // 2, m % 2
                                z = pe.matmul(o, v_pad[b][:, p // 2, h, :], pT[:, m * P:(m + 1) * P],
                                              start=(m == 0), stop=(m == 3))
                        z.then_inc(pv_done, 1)
                if s >= OUT_FIRST:
                    m = sum(OUT_PARTS[:s - OUT_FIRST])
                    out_part(range(m, m + OUT_PARTS[s - OUT_FIRST]))

            for d in range(OUT_UNITS):
                out_unit(U_ATT_OUT, d, OUT_UNITS, att_o,
                         lambda kt, t: pe.wait_ge(o_lo_ready, 2 * (kt // HALF_PAIRS) + t + 1), E_FFN[1],
                         tiles=(0,) if d < 2 else (0, 1))
            ffn(1, E_FFN[2])
            ffn(2, E_GDN)

            def g_transposes(g, f, source):
                t = f % 2
                if f < 2:
                    if g:
                        pe.wait_ge(o_lo_ready, 4 + TT * (g - 1) + t + 1)
                elif f < FILL_A:
                    pe.wait_ge(g_evac_act, EVACS_G * g + t + 1)
                elif f < FILL_X:
                    pe.wait_ge(g_evac_vec, TT * g + t + 1)
                else:
                    pe.wait_ge(g_evac_act, EVACS_G * g + 2 + (f - FILL_X) + 1)
                for h in range(HG):
                    z = pe.transpose(bank[4 + t][:, h * P:(h + 1) * P], source(t, h), ident[:])
                z.then_inc(g_fill, 1)

            def channel_unit(u0, kh, banks, e=None):
                wait_split(pe, u0)
                if e is not None:
                    pe.wait_ge(xT_lo_ready, 4 * e + quarters(e).index((TT - 1, kh)) + 1)
                for h in range(HG):
                    for j in range(4):
                        kt = 4 * kh + j
                        z = products(bank[banks[h // 2]][:, (h % 2) * SEQ:(h % 2 + 1) * SEQ],
                                     ring(u0, slice(j * BANK + h * P, j * BANK + (h + 1) * P)),
                                     (xT_hi[:, kt, :], xT_lo[:, kt, :]),
                                     start=(kt == 0 and h % 2 == 0), stop=(kt == KT - 1),
                                     skip_group_check=True)
                z.then_inc(unit_done, 1)

            def heads(b, a, m, ready=None):
                for h in range(HG):
                    z = pe.matmul(bank[b][:, h * P:(h + 1) * P], a(h), m(h), start=True, stop=True)
                return z

            def half_heads(to, a, m, b, odd):
                for h in range(HG):
                    z = pe.matmul(bank[to][:, h * P // 2:(h + 1) * P // 2].rearrange("p (n b) -> p n b", b=b),
                                  a[:, h, :], block_columns(m[:, h, :], b, odd), start=True, stop=True)
                return z

            def o_transposes(g):
                for t in range(TT):
                    pe.wait_ge(O_final, TT * g + t + 1)
                    g_transposes(g, FILL_O + t, lambda t, h: Lm[t][:, h, :])

            q_T, k_T, v_T = cT
            nl = len(LEVELS)
            for g in range(NG):
                u = U_GDN + 8 * g
                tile = [slice(t * P, (t + 1) * P) for t in range(TT)]
                channel_unit(u, 0, CONV_BANKS[0], E_GDN if g == 0 else None)
                if g:
                    pe.wait_ge(O_ready, TT * g)
                    o_transposes(g - 1)
                channel_unit(u + 1, 1, CONV_BANKS[0], E_GDN if g == 0 else None)
                if g == 0:
                    pe.wait_ge(wba_ready, 1)
                    for kt in range(KT):
                        z = products(bank[6][:, 0:SEQ], (wba_hi[:, kt, :], wba_lo[:, kt, :]),
                                     (xT_hi[:, kt, :], xT_lo[:, kt, :]), start=(kt == 0), stop=(kt == KT - 1))
                    z.then_inc(ba_psum, 1)
                channel_unit(u + 2, 0, CONV_BANKS[1])
                if g == 0:
                    pe.wait_ge(ba_ready, 1)
                    for t in range(TT):
                        z = pe.transpose(bank[7][:, tile[t]], ba_T[:, tile[t]], ident[:])
                    z.then_inc(dec_psum, 1)
                channel_unit(u + 3, 1, CONV_BANKS[1])
                if g == 0:
                    pe.wait_ge(gate_dve, GATE_G)
                    pe.wait_ge(g_masks, 1)
                    n = TT * GH
                    pe.matmul(bank[6][:, 0:n], upper[:], gates[:, 1].rearrange("p t h -> p (t h)"),
                              start=True, stop=True)
                    pe.matmul(bank[6][:, n:2 * n], ones[:], gates[:, 1].rearrange("p t h -> p (t h)"),
                              start=True, stop=True).then_inc(dec_psum, 1)
                pe.wait_ge(conv_ready, 3 * g + 1)
                for t in range(TT):
                    g_transposes(g, t, lambda t, h: q_T[:, h, tile[t]])
                if g == 0:
                    pe.wait_ge(gate_dve, GATE_G + 2)
                for kh in range(2):
                    channel_unit(u + 4 + kh, kh, CONV_BANKS[2])
                pe.wait_ge(conv_ready, 3 * g + 2)
                for t in range(TT):
                    g_transposes(g, FILL_K + t, lambda t, h: k_T[:, h, tile[t]])
                for t in range(TT):
                    pe.wait_ge(gU_ready, TT * g + t + 1)
                    pe.matmul(bank[R_BANK[t]][:], ones[:], gU[:, t].rearrange("p h n -> p (h n)"),
                              start=True, stop=True).then_inc(R_psum, 1)
                for kh in range(2):
                    in_unit(u + 6 + kh, 0, kh, (0, 1))
                pe.wait_ge(decay_diff, TT * (g + 1))
                for t in range(TT):
                    heads(KK_BANK[t], lambda h: k_T[:, h, tile[t]],
                          lambda h: k_T[:, h, tile[t]]).then_inc(KK_psum, 1)
                for t in range(TT):
                    heads(QK_BANK[t], lambda h: q_T[:, h, tile[t]],
                          lambda h: k_T[:, h, tile[t]]).then_inc(QK_psum, 1)
                for t in range(TT):
                    pe.wait_ge(A_ready, TT * g + t + 1)
                    g_transposes(g, FILL_A + t, lambda t, h: Y[t][:, h, :])
                for t in range(TT):
                    pe.wait_ge(X_ready, 2 * nl * g + t + 1)
                    g_transposes(g, FILL_X + t, lambda t, h: X[t][:, h, :])
                for t in range(TT):
                    pe.wait_ge(Aqk_ready, TT * g + t + 1)
                    g_transposes(g, FILL_AQK + t, lambda t, h: Lm[t][:, h, :])
                pe.wait_ge(z_silu, TT * (g + 1))
                for n, b in enumerate(LEVELS):
                    for t in range(TT):
                        pe.wait_ge(X_ready, 2 * nl * g + 2 * n + t + 1)
                        half_heads(Y_BANK[t], AT[t], X[t], b, 0).then_inc(Y_psum, 1)
                        if n:
                            for h in range(HG):
                                z = pe.transpose(bank[ZT_BANK[t]][:, h * P:(h + 1) * P], X[t][:, h, :], ident[:])
                            z.then_inc(XT_psum, 1)
                    if n == 0:
                        pe.wait_ge(conv_ready, 3 * g + 3)
                        for t in range(TT):
                            g_transposes(g, FILL_V + t, lambda t, h: v_T[:, h, tile[t]])
                    for t in range(TT):
                        if n == 0:
                            pe.wait_ge(g_evac_act, EVACS_G * g + 4 + t + 1)
                        else:
                            pe.wait_ge(XT_copied, TT * ((nl - 1) * g + n - 1) + t + 1)
                        pe.wait_ge(Y_ready, 2 * nl * g + 2 * n + t + 1)
                        if n < nl - 1:
                            half_heads(Z_BANK[t], XT[t], Y[t], b, 0).then_inc(Z_psum, 1)
                        else:
                            half_heads(ZT_BANK[t], Y[t], XT[t], b, 1).then_inc(ZT_psum, 1)
                pe.wait_ge(XT_ready, TT * g + 1)
                pe.wait_ge(g_evac_act, EVACS_G * (g + 1))
                heads(U_BANK[0], lambda h: XT[0][:, h, :], lambda h: v_beta[:, 0, h, :]).then_inc(U_psum, 1)
                pe.wait_ge(XT_ready, TT * (g + 1))
                heads(W_BANK, lambda h: k_w[:, h, :], lambda h: XT[1][:, h, :]).then_inc(W_psum, 1)
                pe.wait_ge(U_ready, TT * g + 1)
                heads(S_BANK, lambda h: k_dec[:, h, :], lambda h: Y[0][:, h, :]).then_inc(S_psum, 1)
                heads(O_BANK[0], lambda h: AqkT[0][:, h, :], lambda h: Y[0][:, h, :]).then_inc(O_psum, 1)
                pe.wait_ge(W_ready, g + 1)
                pe.wait_ge(S_ready, g + 1)
                for h in range(HG):
                    o = bank[U_BANK[1]][:, h * P:(h + 1) * P]
                    pe.matmul(o, XT[1][:, h, :], v_beta[:, 1, h, :], start=True, stop=False)
                    z = pe.matmul(o, X[1][:, h, :], X[0][:, h, :], start=False, stop=True)
                z.then_inc(U_psum, 1)
                heads(QS_BANK, lambda h: q_T[:, h, tile[1]], lambda h: X[0][:, h, :]).then_inc(QS_psum, 1)
                pe.wait_ge(U_ready, TT * g + 2)
                heads(O_BANK[1], lambda h: AqkT[1][:, h, :], lambda h: Y[1][:, h, :]).then_inc(O_psum, 1)

            def gdn_o(kt, t):
                at = slice(t * P, (t + 1) * P)
                return g_oT_hi[:, kt, at], g_oT_lo[:, kt, at]

            pe.wait_ge(O_ready, TT * NG - 1)
            for d in range(OUT_UNITS):
                if d == 1:
                    o_transposes(NG - 1)
                out_unit(U_GDN_OUT, d, OUT_UNITS, gdn_o,
                         lambda kt, t: pe.wait_ge(o_lo_ready, 4 + TT * (kt // HG) + t + 1), E_FFN[3])
            ffn(3, 6)

_INS = ["x", "positions", "ffn1_norm", "ffn1_w_gate_up", "ffn1_w_down", "mix_norm", "ffn2_norm",
        "ffn2_w_gate_up", "ffn2_w_down", "attn_w_in", "attn_b_in", "attn_sinks", "attn_w_out",
        "attn_b_out", "gdn_w_in", "gdn_conv_w", "gdn_A_log", "gdn_dt_bias", "gdn_norm_w",
        "gdn_w_out", "final_norm"]
_OUT = (1, SEQ, D)


def kernel(**inputs):
    import concourse.bacc as _bacc
    from concourse.bass_utils import run_bass_kernel_spmd as _run

    nc = _bacc.Bacc("TRN2", target_bir_lowering=False, num_devices=1)
    arrays, args = {}, []
    for name in _INS:
        a = np.ascontiguousarray(inputs[name])
        arrays[f"in_{name}"] = a
        args.append(nc.dram_tensor(f"in_{name}", a.shape, mybir.dt.from_np(a.dtype), kind="ExternalInput").ap())
    args.append(nc.dram_tensor("out_0", _OUT, F32, kind="ExternalOutput").ap())
    build(nc, *args)
    r = _run(nc, [arrays], core_ids=[0])
    return r.results[0]["out_0"]
```
